# Optimizing a Trainium2 kernel written in Bass

```python
import math
import jax, jax.numpy as jnp
from jax import lax
import numpy as np

D_MODEL = 2048
BATCH = 1
SEQ = 256
DEPTH = 1

N_BRANCHES = 3
POOL_WINDOWS = (2, 4, 8, 16)
N_POOL_GROUPS = 4
POOL_DIM = D_MODEL // 2
POOL_GROUP_DIM = POOL_DIM // N_POOL_GROUPS
CONV_DIM = D_MODEL // 2
CONV_WIDTH = 3
N_HEADS = 8
HEAD_DIM = 128
N_KV_HEADS = 2
GROUP = N_HEADS // N_KV_HEADS
ATTN_DIM = N_HEADS * HEAD_DIM
IDX_HEADS = 16
IDX_DIM = 64
TOPK_MAX = 256
Q_BLOCK = 128
NUM_BUCKETS = 32
MAX_EXACT = NUM_BUCKETS // 2
MAX_DISTANCE = 128
BRANCH_DIM = D_MODEL // 2
MLP_HIDDEN = 4 * D_MODEL
NORM_EPS = 1e-6
IN_SPLITS = (POOL_DIM, CONV_DIM, CONV_DIM, CONV_DIM, ATTN_DIM, N_KV_HEADS * HEAD_DIM,
             N_KV_HEADS * HEAD_DIM, IDX_HEADS * IDX_DIM, IDX_DIM, IDX_HEADS)
IN_WIDTH = sum(IN_SPLITS)


def _split_points():
    pts, acc = [], 0
    for w in IN_SPLITS[:-1]:
        acc += w
        pts.append(acc)
    return pts

def rmsnorm(x, g):
    xf = x.astype(jnp.float32)
    y = xf * lax.rsqrt(jnp.mean(jnp.square(xf), axis=-1, keepdims=True) + NORM_EPS)
    return (y * g.astype(jnp.float32)).astype(x.dtype)

def t5_bucket(dist):
    n = jnp.maximum(dist, 0)
    nf = jnp.maximum(n, 1).astype(jnp.float32)
    large = MAX_EXACT + (jnp.log(nf / MAX_EXACT) / math.log(MAX_DISTANCE / MAX_EXACT)
                         * (NUM_BUCKETS - MAX_EXACT)).astype(jnp.int32)
    large = jnp.minimum(large, NUM_BUCKETS - 1)
    return jnp.where(n < MAX_EXACT, n, large)

def pool_mixer(u, pool_w, pool_scale):
    B, S, _ = u.shape
    ug = u.astype(jnp.float32).reshape(B, S, N_POOL_GROUPS, POOL_GROUP_DIM)
    c0 = jnp.concatenate([jnp.zeros((B, 1, N_POOL_GROUPS, POOL_GROUP_DIM), jnp.float32),
                          jnp.cumsum(ug, axis=1)], axis=1)
    t = jnp.arange(S)
    win = jnp.array(POOL_WINDOWS, jnp.int32)
    lo = jnp.maximum(t[:, None] + 1 - win[None, :], 0)
    g_ar = jnp.arange(N_POOL_GROUPS)[None, :]
    window_sum = c0[:, 1:] - c0[:, lo, g_ar]
    cnt = (t[:, None] + 1 - lo).astype(jnp.float32)[None, :, :, None]
    d = window_sum / cnt - ug
    y = jnp.einsum('bsgc,gcd->bsgd', d, pool_w.astype(jnp.float32))
    return (y.reshape(B, S, POOL_DIM) * pool_scale.astype(jnp.float32)).astype(u.dtype)

def conv_mixer(u, gate_c, gate_b, conv_w):
    z = gate_c * u
    y = lax.conv_general_dilated(z, conv_w[:, None, :], window_strides=(1,),
                                 padding=[(CONV_WIDTH - 1, 0)],
                                 dimension_numbers=('NWC', 'WIO', 'NWC'),
                                 feature_group_count=CONV_DIM)
    return gate_b * y

def sparse_attention(q, k, v, q_idx, k_idx, w_idx, rel_bias):
    B, S = q.shape[0], q.shape[1]
    topk = min(TOPK_MAX, S // 4)
    nblk = S // Q_BLOCK
    key_pos = jnp.arange(S)
    k_idx32 = k_idx.astype(jnp.float32)
    table = rel_bias.astype(jnp.float32)

    def to_blocks(a):
        return jnp.moveaxis(a.reshape((B, nblk, Q_BLOCK) + a.shape[2:]), 1, 0)

    def block_fn(args):
        qb, qib, wb, blk = args
        q_pos = blk * Q_BLOCK + jnp.arange(Q_BLOCK)
        dots = jnp.einsum('bthd,bsd->bths', qib.astype(jnp.float32), k_idx32)
        score = jnp.einsum('bth,bths->bts', wb.astype(jnp.float32) * IDX_HEADS ** -0.5,
                           jax.nn.relu(dots))
        causal = key_pos[None, :] <= q_pos[:, None]
        score = jnp.where(causal[None], score, -jnp.inf)
        _, idx = lax.top_k(score, topk)
        k_sel = jax.vmap(lambda kb, ib: kb[ib])(k, idx)
        v_sel = jax.vmap(lambda vb, ib: vb[ib])(v, idx)
        qg = qb.reshape(B, Q_BLOCK, N_KV_HEADS, GROUP, HEAD_DIM).astype(jnp.float32)
        logits = jnp.einsum('btgrd,btkgd->btgrk', qg, k_sel.astype(jnp.float32)) * HEAD_DIM ** -0.5
        dist = q_pos[None, :, None] - idx
        bias = table[t5_bucket(dist)]
        bias = bias.reshape(B, Q_BLOCK, topk, N_KV_HEADS, GROUP).transpose(0, 1, 3, 4, 2)
        logits = jnp.where((dist >= 0)[:, :, None, None, :], logits + bias, -jnp.inf)
        p = jax.nn.softmax(logits, axis=-1)
        o = jnp.einsum('btgrk,btkgd->btgrd', p, v_sel.astype(jnp.float32))
        return o.reshape(B, Q_BLOCK, ATTN_DIM).astype(q.dtype)

    out = lax.map(block_fn, (to_blocks(q), to_blocks(q_idx), to_blocks(w_idx),
                             jnp.arange(nblk, dtype=jnp.int32)))
    return jnp.moveaxis(out, 0, 1).reshape(B, S, ATTN_DIM)

def first_inputs(seed: int = 0) -> dict:
    key = jax.random.key(seed)
    ks = jax.random.split(key, 13)

    def nrm(k, shape, scale):
        return jax.random.normal(k, shape, jnp.float32) * scale

    return {
        'x': nrm(ks[0], (BATCH, SEQ, D_MODEL), 1.0),
        'norm_gains': 1.0 + nrm(ks[1], (DEPTH, 4, D_MODEL), 0.05),
        'w_in': nrm(ks[2], (DEPTH, D_MODEL, IN_WIDTH), D_MODEL ** -0.5),
        'pool_w': nrm(ks[3], (DEPTH, N_POOL_GROUPS, POOL_GROUP_DIM, POOL_GROUP_DIM), POOL_GROUP_DIM ** -0.5),
        'pool_scale': 1.0 + nrm(ks[4], (DEPTH, POOL_DIM), 0.05),
        'conv_w': nrm(ks[5], (DEPTH, CONV_WIDTH, CONV_DIM), CONV_WIDTH ** -0.5),
        'rel_bias': nrm(ks[6], (NUM_BUCKETS, N_HEADS), 0.5),
        'w_branch': nrm(ks[7], (DEPTH, N_BRANCHES, BRANCH_DIM, D_MODEL), BRANCH_DIM ** -0.5),
        'w_gate': nrm(ks[8], (DEPTH, D_MODEL, N_BRANCHES * D_MODEL), D_MODEL ** -0.5),
        'b_gate': nrm(ks[9], (DEPTH, N_BRANCHES, D_MODEL), 0.1),
        'w_out': nrm(ks[10], (DEPTH, D_MODEL, D_MODEL), D_MODEL ** -0.5),
        'w_up': nrm(ks[11], (DEPTH, D_MODEL, MLP_HIDDEN), D_MODEL ** -0.5),
        'w_down': nrm(ks[12], (DEPTH, MLP_HIDDEN, D_MODEL), MLP_HIDDEN ** -0.5),
    }

def first_block(x, norm_gains, w_in, pool_w, pool_scale, conv_w, rel_bias, w_branch,
              w_gate, b_gate, w_out, w_up, w_down):
    B, S, D = x.shape
    pts = _split_points()
    for l in range(DEPTH):
        g = norm_gains[l]
        h = rmsnorm(x, g[0])
        proj = h @ w_in[l]
        (u_pool, u_conv, c_gate, b_gate_conv, q, k, v, qi, ki, wi) = jnp.split(proj, pts, axis=-1)
        y_pool = pool_mixer(u_pool, pool_w[l], pool_scale[l])
        y_conv = conv_mixer(u_conv, c_gate, b_gate_conv, conv_w[l])
        y_attn = sparse_attention(q.reshape(B, S, N_HEADS, HEAD_DIM),
                                  k.reshape(B, S, N_KV_HEADS, HEAD_DIM),
                                  v.reshape(B, S, N_KV_HEADS, HEAD_DIM),
                                  qi.reshape(B, S, IDX_HEADS, IDX_DIM), ki, wi, rel_bias)
        branches = jnp.stack([y_pool, y_conv, y_attn], axis=2)
        up = jnp.einsum('bsnc,ncd->bsnd', branches, w_branch[l])
        gates = jax.nn.sigmoid((h @ w_gate[l]).reshape(B, S, N_BRANCHES, D) + b_gate[l])
        mixed = jnp.sum(gates * up, axis=2) @ w_out[l]
        x = x + rmsnorm(mixed, g[1])
        h = rmsnorm(x, g[2])
        m = jnp.square(jax.nn.relu(h @ w_up[l])) @ w_down[l]
        x = x + rmsnorm(m, g[3])
    return x


CTX_LEN = 256
GRID_W = 64
ATT_W = (3 * D_MODEL) // 4
N_Q_HEADS = ATT_W // HEAD_DIM
N_KV_HEADS_2 = 4
Q_PER_KV = N_Q_HEADS // N_KV_HEADS_2
KV_W = N_KV_HEADS_2 * HEAD_DIM
FNET_W = D_MODEL // 4
N_FNET_GROUPS = 4
FNET_GROUP = FNET_W // N_FNET_GROUPS
ROPE_THETA = 10000.0
ROPE_AXIS_DIM = HEAD_DIM // 2
ROPE_NFREQ = ROPE_AXIS_DIM // 2
EPS = 1e-6

OFF_Q = 0
OFF_K = OFF_Q + ATT_W
OFF_V = OFF_K + KV_W
OFF_ZA = OFF_V + KV_W
OFF_UB = OFF_ZA + ATT_W
OFF_ZB = OFF_UB + FNET_W
OFF_GA = OFF_ZB + FNET_W
OFF_GB = OFF_GA + D_MODEL
IN_W = OFF_GB + D_MODEL
R_ZA = 0
R_UB = OFF_UB - OFF_ZA
R_ZB = OFF_ZB - OFF_ZA
R_GA = OFF_GA - OFF_ZA
R_GB = OFF_GB - OFF_ZA


def _rmsnorm(x, g):
    xf = x.astype(jnp.float32)
    y = xf * lax.rsqrt(jnp.mean(xf * xf, axis=-1, keepdims=True) + EPS)
    return (y * g.astype(jnp.float32)).astype(x.dtype)

def _modulate(h, shift, scale):
    return h * (1 + scale) + shift

def _heads(p, lo, n_heads):
    b, n, _ = p.shape
    return p[..., lo:lo + n_heads * HEAD_DIM].reshape(b, n, n_heads, HEAD_DIM)

def _axial_rope_tables(n_tokens):
    rows = n_tokens // GRID_W
    row_pos = jnp.repeat(jnp.arange(rows, dtype=jnp.float32), GRID_W)
    col_pos = jnp.tile(jnp.arange(GRID_W, dtype=jnp.float32), rows)
    inv = ROPE_THETA ** (-jnp.arange(ROPE_NFREQ, dtype=jnp.float32) / ROPE_NFREQ)
    ang = jnp.stack([row_pos[:, None] * inv, col_pos[:, None] * inv], axis=1)
    return jnp.cos(ang), jnp.sin(ang)

def _rope(x, cos, sin):
    b, n, h, _ = x.shape
    xf = x.astype(jnp.float32).reshape(b, n, h, 2, 2, ROPE_NFREQ)
    x1, x2 = xf[..., 0, :], xf[..., 1, :]
    cc, ss = cos[None, :, None], sin[None, :, None]
    out = jnp.stack([x1 * cc - x2 * ss, x2 * cc + x1 * ss], axis=-2)
    return out.reshape(b, n, h, HEAD_DIM).astype(x.dtype)

def _attention(q, k, v):
    b, n = q.shape[:2]
    nblk = n // Q_BLOCK
    qb = q.reshape(b, nblk, Q_BLOCK, N_KV_HEADS_2, Q_PER_KV, HEAD_DIM).transpose(1, 0, 2, 3, 4, 5)

    def block(qi):
        s = jnp.einsum('bqhgd,bkhd->bhgqk', qi, k, preferred_element_type=jnp.float32)
        w = jax.nn.softmax(s, axis=-1).astype(v.dtype)
        return jnp.einsum('bhgqk,bkhd->bqhgd', w, v)

    o = lax.map(block, qb)
    return o.transpose(1, 0, 2, 3, 4, 5).reshape(b, n, ATT_W)

def _fourier_mix(u):
    b, n, _ = u.shape
    ug = u.astype(jnp.float32).reshape(b, n, N_FNET_GROUPS, FNET_GROUP)
    y = jnp.fft.fftn(ug, axes=(1, 3), norm="ortho").real
    return y.reshape(b, n, FNET_W).astype(u.dtype)

def _merge(p_rest, attn, w_pa, w_pb, w_o):
    z_a = p_rest[..., R_ZA:R_UB]
    u_b = p_rest[..., R_UB:R_ZB]
    z_b = p_rest[..., R_ZB:R_GA]
    g_a = jax.nn.sigmoid(p_rest[..., R_GA:R_GB])
    g_b = jax.nn.sigmoid(p_rest[..., R_GB:])
    y_a = (attn * jax.nn.silu(z_a)) @ w_pa
    y_b = (_fourier_mix(u_b) * jax.nn.silu(z_b)) @ w_pb
    return (g_a * y_a + g_b * y_b) @ w_o

def second_inputs(seed: int = 0) -> dict:
    key = jax.random.key(seed)
    ks = jax.random.split(key, 16)
    f32 = jnp.float32
    nrm = lambda k, shape, s: jax.random.normal(k, shape, f32) * s
    return {
        "x": nrm(ks[0], (BATCH, SEQ, D_MODEL), 1.0),
        "c": nrm(ks[1], (BATCH, D_MODEL), 1.0),
        "ctx": nrm(ks[2], (BATCH, CTX_LEN, D_MODEL), 1.0),
        "c_ctx": nrm(ks[3], (D_MODEL,), 1.0),
        "w_ada": nrm(ks[4], (DEPTH, D_MODEL, 3 * D_MODEL), D_MODEL ** -0.5),
        "b_ada": nrm(ks[5], (DEPTH, 3 * D_MODEL), 0.01),
        "norm_g": 1.0 + nrm(ks[6], (DEPTH, D_MODEL), 0.01),
        "w_in": nrm(ks[7], (DEPTH, D_MODEL, IN_W), D_MODEL ** -0.5),
        "q_norm_g": 1.0 + nrm(ks[8], (DEPTH, HEAD_DIM), 0.01),
        "k_norm_g": 1.0 + nrm(ks[9], (DEPTH, HEAD_DIM), 0.01),
        "w_proj_a": nrm(ks[10], (DEPTH, ATT_W, D_MODEL), ATT_W ** -0.5),
        "w_proj_b": nrm(ks[11], (DEPTH, FNET_W, D_MODEL), FNET_W ** -0.5),
        "w_out": nrm(ks[12], (DEPTH, D_MODEL, D_MODEL), D_MODEL ** -0.5),
        "final_g": 1.0 + nrm(ks[13], (D_MODEL,), 0.01),
    }

def second_block(x, c, ctx, c_ctx, w_ada, b_ada, norm_g, w_in, q_norm_g, k_norm_g,
              w_proj_a, w_proj_b, w_out, final_g):
    n_lat = x.shape[1]
    cos, sin = _axial_rope_tables(n_lat)
    q_scale = HEAD_DIM ** -0.5
    silu_c = jax.nn.silu(c)
    silu_cc = jax.nn.silu(c_ctx)
    xs, cs = x, ctx
    for l in range(DEPTH):
        last = l == DEPTH - 1
        w_l = w_in[l]
        shift, scale, gate = jnp.split(silu_c @ w_ada[l] + b_ada[l], 3, axis=-1)
        shift_c, scale_c, gate_c = jnp.split(silu_cc @ w_ada[l] + b_ada[l], 3, axis=-1)
        h = _modulate(_rmsnorm(xs, norm_g[l]), shift[:, None], scale[:, None])
        hc = _modulate(_rmsnorm(cs, norm_g[l]), shift_c, scale_c)

        pc_kv = hc @ w_l[:, OFF_K:OFF_ZA]
        kc = _rmsnorm(_heads(pc_kv, 0, N_KV_HEADS_2), k_norm_g[l])
        vc = _heads(pc_kv, KV_W, N_KV_HEADS_2)

        p = h @ w_l
        q = _rope(_rmsnorm(_heads(p, OFF_Q, N_Q_HEADS), q_norm_g[l]), cos, sin) * q_scale
        k = _rope(_rmsnorm(_heads(p, OFF_K, N_KV_HEADS_2), k_norm_g[l]), cos, sin)
        v = _heads(p, OFF_V, N_KV_HEADS_2)
        attn = _attention(q, jnp.concatenate([k, kc], axis=1), jnp.concatenate([v, vc], axis=1))
        y = _merge(p[..., OFF_ZA:], attn, w_proj_a[l], w_proj_b[l], w_out[l])
        new_xs = xs + gate[:, None] * y

        if not last:
            qc = _rmsnorm(_heads(hc @ w_l[:, OFF_Q:OFF_K], 0, N_Q_HEADS), q_norm_g[l]) * q_scale
            attn_c = _attention(qc, kc, vc)
            yc = _merge(hc @ w_l[:, OFF_ZA:], attn_c, w_proj_a[l], w_proj_b[l], w_out[l])
            cs = cs + gate_c * yc
        xs = new_xs
    return _rmsnorm(xs, final_g)


def setup_inputs(seed=0):
    out = dict(first_inputs(seed))
    for name, value in second_inputs(seed + 1).items():
        if name != "x":
            out[name + "_2"] = value
    return out


def reference(
    x, norm_gains, w_in, pool_w, pool_scale, conv_w, rel_bias, w_branch, w_gate, b_gate, w_out,
    w_up, w_down, c_2, ctx_2, c_ctx_2, w_ada_2, b_ada_2, norm_g_2, w_in_2, q_norm_g_2,
    k_norm_g_2, w_proj_a_2, w_proj_b_2, w_out_2, final_g_2,
):
    x = first_block(
        x, norm_gains, w_in, pool_w, pool_scale, conv_w, rel_bias, w_branch, w_gate, b_gate,
        w_out, w_up, w_down,
    )
    return second_block(
        x, c_2, ctx_2, c_ctx_2, w_ada_2, b_ada_2, norm_g_2, w_in_2, q_norm_g_2, k_norm_g_2,
        w_proj_a_2, w_proj_b_2, w_out_2, final_g_2,
    )


_drawn_inputs = setup_inputs


def setup_inputs(seed=0):
    import zlib

    import numpy as np

    out = dict(_drawn_inputs(seed))
    spreads = {}
    factors = {'ctx_2': 5.758,
     'b_ada_2': 8.0,
     'norm_g_2': 8.0,
     'q_norm_g_2': 8.0,
     'k_norm_g_2': 8.0,
     'final_g_2': 5.563}
    for name, (base, spread) in spreads.items():
        noise = np.random.default_rng([zlib.crc32(name.encode()), seed]).standard_normal(out[name].shape)
        drawn = base * np.exp(spread * noise) if base else spread * noise
        out[name] = __import__('jax').numpy.asarray(drawn.astype(out[name].dtype))
    for name, factor in factors.items():
        out[name] = (out[name] * factor).astype(out[name].dtype)
    return out
```

```python
import math
from contextlib import ExitStack

import numpy as np

import concourse.bass as bass
from concourse import mybir
from concourse.alu_op_type import AluOpType as ALU

ACT = mybir.ActivationFunctionType
AX = mybir.AxisListType.X
F32 = mybir.dt.float32
F32R = mybir.dt.float32r

D = 2048
EPS = 1e-6
HID = 8192
KC = 2
NRAW = 6
NSPL = 4
AHEAD = 3
ATT_SCALE = 128 ** -0.5
BIG = 1e30
PE, AC, DV, PO, SP = "pe", "act", "dve", "pool", "sp"


def constants():
    t = np.arange(256)
    pm = np.zeros((256, 4, 256), np.float64)
    for g, w in enumerate((2, 4, 8, 16)):
        for i in t:
            lo = max(i + 1 - w, 0)
            pm[lo:i + 1, g, i] = 1.0 / (i + 1 - lo)
            pm[i, g, i] -= 1.0
    pm = pm.reshape(2, 128, 4 * 256).transpose(1, 0, 2).reshape(128, 2048)
    onehot = np.zeros((32, 384), np.float32)
    for j in range(384):
        d = 255 - j
        if d >= 0:
            b = d if d < 16 else min(16 + int(math.log(d / 16) / math.log(8) * 16), 31)
            onehot[b, j] = 1.0
    cm = np.where(t[None, :] <= t[:, None], 0.0, -BIG)
    cm = cm.reshape(2, 128, 256).transpose(1, 0, 2).reshape(128, 512)
    inv = np.float32(10000.0) ** (-np.arange(32, dtype=np.float32) / np.float32(32))
    ang = np.stack([(t // 64).astype(np.float32)[:, None] * inv, (t % 64).astype(np.float32)[:, None] * inv], 1)
    co, si = np.cos(ang.astype(np.float64)), np.sin(ang.astype(np.float64))
    rc = np.tile(np.stack([co, co], 2).reshape(256, 128), (1, 4))
    rs = np.tile(np.stack([-si, si], 2).reshape(256, 128), (1, 4))
    rc = rc.reshape(2, 128, 512).transpose(1, 0, 2).reshape(128, 1024)
    rs = rs.reshape(2, 128, 512).transpose(1, 0, 2).reshape(128, 1024)
    a = 2 * np.pi * (np.outer(t, t) % 256) / 256
    cs = np.concatenate([np.cos(a), np.sin(a)], 1).reshape(2, 128, 512).transpose(1, 0, 2).reshape(128, 1024)
    d = np.arange(128)
    b = 2 * np.pi * (np.outer(d, d) % 128) / 128
    cd = np.concatenate([np.cos(b), -np.sin(b)], 1) / math.sqrt(256 * 128)
    s5 = np.zeros((5, 130), np.float32)
    s5[:, 0] = (1, 0, 1, 0, 1)
    s5[:, 1] = (0, 1, 0, 1, 1)
    s5[:, 2:] = s5[:, 0:1]
    f = {"k_ident": np.eye(128), "k_flip": np.eye(128)[::-1], "k_pm": pm, "k_onehot": onehot, "k_cm": cm, "k_rc": rc, "k_rs": rs,
         "k_cs": cs, "k_cd": cd, "k_s5": s5}
    return {n: np.ascontiguousarray(v, dtype=np.float32) for n, v in f.items()}


class Program:

    def __init__(self, nc, ctx):
        self.nc, self.ctx = nc, ctx
        self.q = {e: [] for e in (PE, AC, DV, PO, SP)}
        self.seen = {e: {} for e in self.q}
        self.count = {}
        self.sems = {}
        for e in (PE, AC, DV, PO):
            self.new_sem(e)

    def new_sem(self, name):
        self.sems[name] = self.ctx.enter_context(self.nc.semaphore("s_" + name))
        self.count[name] = 0
        return name

    def wait(self, eng, *tokens):
        for t in tokens:
            if t is None:
                continue
            if isinstance(t, list):
                self.wait(eng, *t)
                continue
            name, value = t
            if self.seen[eng].get(name, 0) < value:
                self.seen[eng][name] = value
                s = self.sems[name]
                self.q[eng].append(lambda e, s=s, v=value: e.wait_ge(s, v))

    def op(self, eng, fn, *tokens):
        self.wait(eng, *tokens)
        self.count[eng] += 1
        s = self.sems[eng]
        self.q[eng].append(lambda e: fn(e).then_inc(s, 1))
        return (eng, self.count[eng])

    def quiet(self, eng, fn, *tokens):
        self.wait(eng, *tokens)
        self.q[eng].append(fn)

    def dma(self, eng, sem, dst, src, *tokens):
        self.wait(eng, *tokens)
        self.count[sem] += 16
        s = self.sems[sem]
        self.q[eng].append(lambda e: e.dma_start(dst, src).then_inc(s, 16))
        return (sem, self.count[sem])


class Pool:

    def __init__(self, bufs):
        self.free = [(b, []) for b in bufs]

    def put(self, b, *tokens):
        self.free.append((b, list(tokens)))


class Operand:

    def __init__(self, hi, lo):
        self.hi, self.lo = hi, lo
        self.read = None
        self.ready = {}


class Job:
    def __init__(self, mode, op, w, kt0, nkt, cols, epilogue, need=(), gate=None):
        self.mode, self.op, self.w, self.kt0, self.nkt, self.cols = mode, op, w, kt0, nkt, cols
        self.epilogue, self.need = epilogue, need
        self.n = sum(c[1] for c in cols)
        self.banks = None


def program(nc, a, out, scratch_e, scratch_x):
    ctx = ExitStack()
    with ctx:
        ctx.enter_context(nc.allow_low_precision("float32 values are kept in two exact float32r parts"))
        p = Program(nc, ctx)
        base = nc.sbuf_base
        top = [(base + 63) // 64 * 64]

        def at(name, shape, off, dt=F32):
            return nc.alloc_sbuf_tensor_at(name, shape, dt, offset=off)

        def sb(name, shape, dt=F32):
            size = 4 * int(np.prod(shape[1:]))
            t = at(name, shape, top[0], dt)
            top[0] += (size + 31) // 32 * 32
            return t

        raw = [sb(f"raw{i}", [128, KC, 512]) for i in range(NRAW)]
        whi = [sb(f"whi{i}", [128, KC, 512], F32R) for i in range(NSPL)]
        wlo = [sb(f"wlo{i}", [128, KC, 512], F32R) for i in range(NSPL)]
        op0_at = top[0]
        OP0 = Operand(sb("op0h", [128, 16, 256], F32R), sb("op0l", [128, 16, 256], F32R))
        op1_at = top[0]
        OP1 = Operand(sb("op1h", [128, 16, 256], F32R), sb("op1l", [128, 16, 256], F32R))
        tmp = Pool([sb(f"tmp{i}", [128, 512]) for i in range(4)])
        ident = sb("ident", [128, 128])
        vat = sb("vat", [128, 112])
        vbt = sb("vbt", [128, 82])
        c4 = sb("c4", [128, 188], F32R)
        csil = sb("csil", [128, 32])
        abt = sb("abt", [128, 32, 2])
        acol = sb("acol", [128, 16, 2])
        a5 = sb("a5", [128, 512])
        s5 = sb("s5", [128, 130])
        gqk = sb("gqk", [128, 2, 128])
        mhalf = sb("mhalf", [128, 4])
        stat = sb("stat", [128, 420])
        ss_all = sb("ss_all", [128, 3, 2, 4])
        big = top[0]
        assert big + 72 * 1024 <= nc.sbuf_usable_end, (big, nc.sbuf_usable_end)

        def bg(name, shape, kb, dt=F32):
            return at(name, shape, big + int(kb * 1024), dt)

        qb = bg("qb", [128, 8, 256], 0)
        kt1 = bg("kt1", [128, 2, 256], 8)
        kid = bg("kid", [128, 256], 10)
        v1 = bg("v1", [128, 2, 256], 11)
        wi = bg("wi", [128, 2, 16], 13)
        bt = bg("bt", [128, 8, 256], 14)
        pm = bg("pm", [128, 2, 4, 256], 14)
        sc = bg("sc", [128, 2, 256], 22)
        wk = bg("wk", [128, 2, 256], 24)
        mk = bg("mk", [128, 2, 256], 26)
        mx = bg("mx", [128, 16, 256], 28)
        pu = bg("pu", [128, 2, 512], 28)
        cu = bg("cu", [128, 4, 256], 32)
        pw = bg("pw", [128, 4, 2, 256], 36)
        junk0 = bg("junk0", [128, 2048], 36)
        cz = bg("cz", [128, 4, 258], 44)
        gt = [bg(f"gt{i}", [128, 4, 256], 44 + 4 * i) for i in range(2)]
        x0 = bg("x0", [128, 2, 2048], 52)
        YA = Operand(bg("yah", [128, 8, 256], 52, F32R), bg("yal", [128, 8, 256], 60, F32R))
        cm = bg("cm", [128, 2, 256], 68)
        oneh = bg("oneh", [128, 384], 70)
        flip = bg("flip", [128, 128], 70)
        vst = bg("vst", [128, 128], 71.5)
        erow = bg("erow", [128, 384], 22)
        ktc = bg("ktc", [128, 4, 256], 0)
        vc = bg("vc", [128, 2, 512], 4)
        X = bg("X", [128, 2, 2048], 8)
        macc = bg("macc", [128, 2, 2048], 24)
        HC = Operand(bg("hch", [128, 16, 256], 40, F32R), bg("hcl", [128, 16, 256], 56, F32R))
        g1b = bg("g1b", [128, 2048], 40)
        junk1 = bg("junk1", [128, 2048], 48)
        g3b = at("g3b", [128, 2048], op1_at)
        junk3 = at("junk3", [128, 2048], op1_at + 8192)
        zs = bg("zs", [128, 16, 256], 8)
        qt = bg("qt", [128, 12, 256], 24)
        ktx = bg("ktx", [128, 4, 256], 36)
        vx = bg("vx", [128, 2, 512], 40)
        rct = bg("rct", [128, 2, 512], 44)
        rst = bg("rst", [128, 2, 512], 48)
        ub = bg("ub", [128, 2, 512], 52)
        cst = bg("cst", [128, 2, 512], 56)
        cdt = bg("cdt", [128, 2, 128], 60)
        MG = Operand(bg("mgh", [128, 16, 256], 24, F32R), bg("mgl", [128, 16, 256], 40, F32R))
        ga = [bg(f"ga{i}", [128, 4, 256], 56 + 4 * i) for i in range(2)]
        gb = [bg(f"gb{i}", [128, 4, 256], 64 + 4 * i) for i in range(2)]
        gbc = bg("gbc", [128, 2048], 0)
        X2 = bg("X2", [128, 2, 2048], 8)
        fgb = at("fgb", [128, 2048], op1_at)
        junk2 = at("junk2", [128, 2048], op1_at + 8192)

        bank = [ctx.enter_context(nc.psum_tensor(f"ps{i}", [128, 512], F32)) for i in range(8)]
        main = Pool([(bank[0], bank[1]), (bank[2], bank[3])])
        side = Pool([bank[4]])
        rows = Pool([0])
        misc = Pool([bank[5], bank[6], bank[7]])

        raw_sem = [p.new_sem(f"raw{i}") for i in range(NRAW)]
        R = {}
        tasks = []
        statn = [0]

        def load(name, dst, src, *tokens, eng=PO):
            R[name] = p.dma(eng, p.new_sem("d_" + name), dst, src, *tokens)
            return R[name]

        def col(n=2):
            i = statn[0]
            statn[0] += n
            assert statn[0] <= 420
            return stat[:, i:i + n]

        def step():
            for t in list(tasks):
                if t[1] > 0:
                    t[1] -= 1
                    continue
                try:
                    n = next(t[0])
                    t[1] = (n or 1) - 1
                except StopIteration:
                    tasks.remove(t)

        def until(cond, what=""):
            n = 0
            while not cond():
                step()
                n += 1
                assert n < 500, ("never ready", what)

        def start(gen):
            t = [gen, 0]
            try:
                n = next(gen)
                t[1] = (n or 1) - 1
                tasks.append(t)
            except StopIteration:
                pass

        def take(pool):
            while not pool.free:
                yield 1
            return pool.free.pop(0)

        def have(*names):
            while not all(n in R for n in names):
                yield 1

        def split(src, tok, hi, lo, *war, fast=False):
            if fast:
                t = p.op(DV, lambda e: e.tensor_copy(hi, src), tok, *war)
            else:
                t = p.op(AC, lambda e: e.activation(hi, src, ACT.Copy), tok, *war)
            return p.op(DV, lambda e: e.tensor_tensor(lo, src, hi.bitcast(F32), ALU.subtract), t, tok, *war)

        def rstd(dst, ss, tok, n=D):
            t = p.op(DV, lambda e: e.tensor_scalar(dst, ss, 1.0 / n, EPS, ALU.mult, ALU.add), tok)
            k = dst.shape[-1]
            return p.op(PO, lambda e: e.tensor_tensor(dst, dst, mhalf[:, 0:k], ALU.pow), t, R["mhalf"])

        def norm_rows(src, dst, junk, tok, *war):
            done = []
            sq = None
            for tt in range(2):
                s = col()
                t = sq = p.op(AC, lambda e, tt=tt, s=s: e.activation(junk, src[:, tt, :], ACT.Square, accum_out=s[:, 0:1]), tok[tt],
                              *war, sq)
                t = rstd(s[:, 1:2], s[:, 0:1], t)
                done.append(p.op(DV, lambda e, tt=tt, s=s: e.tensor_scalar(dst[:, tt, :], src[:, tt, :], s[:, 1:2], None, ALU.mult), t, *war))
            return done

        def to_operand(src, toks, a_of, b_of, op, *war, last=None):
            for kp in range(8):
                ps, fr = yield from take(misc)
                for i in range(4):
                    kt, tt = 2 * kp + i // 2, i % 2
                    f = lambda e, kt=kt, tt=tt, i=i, ps=ps: e.transpose(
                        ps[:, i * 128:(i + 1) * 128], src[:, tt, kt * 128:(kt + 1) * 128], ident[:, :])
                    if i < 3:
                        p.quiet(PE, f, fr, toks, R["ident"])
                    else:
                        t = p.op(PE, f, fr, toks, R["ident"])
                tm, ftm = yield from take(tmp)
                for j in range(2):
                    kt = 2 * kp + j
                    b = 0.0 if b_of is None else b_of(kt)
                    u = p.op(AC, lambda e, j=j, kt=kt, ps=ps, tm=tm, b=b: e.activation(
                        tm[:, j * 256:(j + 1) * 256], ps[:, j * 256:(j + 1) * 256], ACT.Identity,
                        bias=b, scale=a_of(kt)), t, ftm)
                misc.put(ps, u)
                src2 = tm[:, :].rearrange("p (k t) -> p k t", k=2)
                z = split(src2, u, op.hi[:, 2 * kp:2 * kp + 2, :], op.lo[:, 2 * kp:2 * kp + 2, :], op.read, *war, fast=True)
                tmp.put(tm, z)
                op.ready[2 * kp] = op.ready[2 * kp + 1] = z
                if kp % 2:
                    yield 1
            if last:
                R[last] = t

        R["mhalf"] = p.op(PO, lambda e: e.memset(mhalf[:, :], -0.5))
        load("va1", vst[0:64, :], a["norm_gains"].rearrange("l g (r c) -> (l g r) c", c=128), eng=SP)
        load("va2", vst[64:112, :], a["b_gate"].rearrange("l g (r c) -> (l g r) c", c=128), eng=SP)
        load("ident", ident[:, :], a["k_ident"], eng=SP)
        load("x0", x0[:, :, :], a["x"].rearrange("b (t p) n -> p (b t) n", p=128), eng=SP)
        load("s5", s5[0:5, :], a["k_s5"])
        load("cm", cm[:, :, :], a["k_cm"].rearrange("p (t s) -> p t s", t=2))
        load("gq", gqk[:, 0, :], a["q_norm_g_2"].partition_broadcast(128).rearrange("p a n -> p (a n)"))
        load("gk", gqk[:, 1, :], a["k_norm_g_2"].partition_broadcast(128).rearrange("p a n -> p (a n)"))
        vec_rows = [("pool_scale", 8, "l (r c) -> (l r) c"), ("conv_w", 24, "l k (r c) -> (l k r) c"),
                    ("norm_g_2", 16, "l (r c) -> (l r) c"), ("q_norm_g_2", 1, None), ("k_norm_g_2", 1, None),
                    ("c_2", 16, "l (r c) -> (l r) c"), ("c_ctx_2", 16, "(r c) -> r c")]
        PS0, CW0, NG0, CC0 = 0, 8, 32, 50

        def setup():
            ps, fr = yield from take(misc)
            t = p.op(PE, lambda e: e.transpose(ps[:, 0:112], vst[0:112, :], ident[0:112, 0:112]), R["va1"], R["va2"], R["ident"])
            R["vat"] = p.op(DV, lambda e: e.tensor_copy(vat[:, :], ps[:, 0:112]), t)
            r0 = 0
            tk = []
            for name, n, pat in vec_rows:
                src = a[name] if pat is None else a[name].rearrange(pat, c=128)
                tk.append(load("vb_" + name, vst[r0:r0 + n, :], src, t, eng=SP))
                r0 += n
            t = p.op(PE, lambda e: e.transpose(ps[:, 128:128 + 82], vst[0:82, :], ident[0:82, 0:82]), R["vat"], *tk)
            R["vbt"] = p.op(DV, lambda e: e.tensor_copy(vbt[:, :], ps[:, 128:128 + 82]), t)
            misc.put(ps, R["vbt"])
            z = p.op(DV, lambda e: e.memset(c4[:, :].bitcast(F32), 0.0))
            t = p.op(AC, lambda e: e.activation(csil[:, :], vbt[:, CC0:CC0 + 32], ACT.Sigmoid), R["vbt"])
            t = p.op(DV, lambda e: e.tensor_tensor(csil[:, :], csil[:, :], vbt[:, CC0:CC0 + 32], ALU.mult), t)
            cv = c4[:, 0:64].rearrange("p (k f) -> p f k", f=4)
            sv = csil[:, :].rearrange("p (f k) -> p f k", f=2)
            t = p.op(DV, lambda e: e.tensor_copy(cv[:, 0:2, :], sv), t, z)
            R["c4"] = p.op(DV, lambda e: e.tensor_tensor(cv[:, 2:4, :], sv, cv[:, 0:2, :].bitcast(F32), ALU.subtract), t)
            xn = norm_rows(x0, x0, junk0[:, :], [R["x0"]] * 2)
            yield from to_operand(x0, xn, lambda kt: vat[:, kt:kt + 1], None, OP0, R["vat"], last="x0T")

        def done(job, *tokens):
            main.put(job.banks, *tokens)

        def ada(j):
            def run(job, t):
                b = job.banks
                if j >= 8:
                    yield from have("attn2")
                _, fa = yield from take(rows)
                tb = p.dma(PO, "d_a5", a5[4:5, :], a["b_ada_2"][0:1, 512 * j:512 * j + 512], fa)
                u = p.op(DV, lambda e: e.tensor_copy(a5[0:4, :], b[0:4, :]), t, fa)
                side.put(b, u)
                yield 1
                ps, fr = yield from take(misc)
                if j < 8:
                    for m in range(4):
                        f = lambda e, m=m, ps=ps: e.matmul(ps[:, 2 * m:2 * m + 2], a5[0:5, 128 * m:128 * m + 128], s5[0:5, 0:2], start=True, stop=True)
                        t = p.op(PE, f, fr, u, tb, R["s5"])
                    v = p.op(DV, lambda e: e.tensor_copy(abt[:, 4 * j:4 * j + 4, :], ps[:, 0:8].rearrange("p (m f) -> p m f", m=4)), t)
                else:
                    t = p.op(PE, lambda e: e.matmul(ps[:, :], s5[0:5, 2:130], a5[0:5, :], start=True, stop=True), fr, u, tb, R["s5"])
                    o = gbc[:, 512 * (j - 8):512 * (j - 7)]
                    v = p.op(DV, lambda e: e.tensor_copy(o, ps[:, :]), t, R["attn2"])
                rows.put(0, t)
                R[f"ada{j}"] = v
                misc.put(ps, v)
                if j == 7:
                    n = vbt[:, NG0:NG0 + 16]
                    for f in range(2):
                        v = p.op(DV, lambda e, f=f: e.scalar_tensor_tensor(acol[:, :, f], abt[:, 16:32, f], 1.0, n, ALU.add, ALU.mult), v, R["vbt"])
                    R["acol"] = v
            return run

        def ev_copy(dst, name, *war):
            def run(job, t):
                nm = job.n // 128
                out_t = []
                for b in range((nm + 1) // 2):
                    k = min(2, nm - 2 * b)
                    o = dst[:, 2 * b:2 * b + k, :]
                    s = job.banks[b][:, 0:256 * k].rearrange("p (k t) -> p k t", k=k)
                    w = [R[x] for x in war]
                    if b % 2:
                        out_t.append(p.op(DV, lambda e, o=o, s=s: e.tensor_copy(o, s), t, w))
                    else:
                        out_t.append(p.op(AC, lambda e, o=o, s=s: e.activation(o, s, ACT.Copy), t, w))
                R[name] = out_t
                done(job, out_t)
                return
                yield
            return run

        def ep_kk(job, t):
            b0, b1 = job.banks
            u = p.op(AC, lambda e: e.activation(kt1[:, :, :], b0[:, :].rearrange("p (k t) -> p k t", k=2), ACT.Copy), t)
            v = p.op(AC, lambda e: e.activation(kid[:, :], b1[:, 0:256], ACT.Copy), t)
            R["k1"] = v
            done(job, v)
            return
            yield

        def ep_vw(job, t):
            o = []
            for tt in range(2):
                b = job.banks[tt]
                o.append(p.op(AC, lambda e, b=b, tt=tt: e.activation(v1[:, tt, :], b[:, 0:256], ACT.Copy), t))
                o.append(p.op(DV, lambda e, b=b, tt=tt: e.tensor_scalar(wi[:, tt, :], b[:, 256:272], 0.25, None, ALU.mult), o[-1]))
            R["v1"] = o
            done(job, o)
            start(indexer())
            return
            yield

        def indexer():
            yield from have("qi0", "qi1", "k1", "v1", "cm")
            first = [True, True]
            last = [None, None]
            units = [(1, par, i) for par in range(2) for i in range(4)] + [(0, par, i) for par in range(2) for i in range(2)]
            for tt, par, i in units:
                nh, nk = (2, 256) if tt else (4, 128)
                hs = [par + 2 * (nh * i + j) for j in range(nh)]
                ps, fr = yield from take(misc)
                for j, h in enumerate(hs):
                    lo = 64 * par
                    f = lambda e, j=j, h=h, ps=ps, lo=lo, tt=tt, nk=nk: e.matmul(
                        ps[:, j * nk:(j + 1) * nk], qb[lo:lo + 64, h // 2, tt * 128:tt * 128 + 128], kid[lo:lo + 64, 0:nk],
                        start=True, stop=True)
                    t = p.op(PE, f, fr, R["qi0"], R["qi1"], R["k1"])
                yield 1
                tm, ftm = yield from take(tmp)
                u = p.op(AC, lambda e, tm=tm, ps=ps: e.activation(tm[:, :], ps[:, :], ACT.Relu), t, ftm)
                misc.put(ps, u)
                for j, h in enumerate(hs):
                    s, r, w = sc[:, tt, 0:nk], tm[:, j * nk:(j + 1) * nk], wi[:, tt, h:h + 1]
                    if first[tt]:
                        first[tt] = False
                        v = p.op(DV, lambda e, s=s, r=r, w=w: e.tensor_scalar(s, r, w, None, ALU.mult), u, R["v1"])
                    else:
                        v = p.op(DV, lambda e, s=s, r=r, w=w: e.scalar_tensor_tensor(s, r, w, s, ALU.mult, ALU.add), u, last[tt])
                    last[tt] = v
                tmp.put(tm, v)
                R["qi_read"] = t
                yield 1
            R["qi_done"] = t
            for tt in range(2):
                nk = 128 * (tt + 1)
                s, w, m = sc[:, tt, 0:nk], wk[:, tt, 0:nk], mk[:, tt, 0:nk]
                c = cm[:, tt, 0:nk]
                v = p.op(DV, lambda e, s=s, c=c: e.tensor_tensor(s, s, c, ALU.add), last[tt])
                for r in range(8):
                    m8 = col(8)
                    i, o = (s, w) if r % 2 == 0 else (w, s)
                    v = p.op(DV, lambda e, m8=m8, i=i: e.max(m8, i), v)
                    v = p.op(DV, lambda e, m8=m8, i=i, o=o: e.match_replace(o, m8, i, -3e38), v)
                    if r % 2:
                        yield 1
                v = p.op(DV, lambda e, s=s, m=m: e.tensor_scalar(m, s, -2e38, BIG, ALU.is_le, ALU.mult), v)
                v = p.op(DV, lambda e, c=c, m=m: e.scalar_tensor_tensor(m, m, -BIG, c, ALU.add, ALU.add), v)
            R["mk"] = v

        def bias_table():
            load("oneh", oneh[0:32, :], a["k_onehot"])
            yield from take(rows)
            rb = load("relb", a5[0:32, 0:8], a["rel_bias"])
            ps, fr = yield from take(misc)
            t = p.op(PE, lambda e: e.matmul(ps[0:8, 0:384], a5[0:32, 0:8], oneh[0:32, :], start=True, stop=True), fr, rb, R["oneh"])
            rows.put(0, t)
            v = p.op(DV, lambda e: e.tensor_copy(erow[0:8, :], ps[0:8, 0:384]), t)
            misc.put(ps, v)
            w = load("erow", scratch_e, erow[0:8, :], v)
            R["erow_w"] = w
            R["erow_m"] = t

        def pool_ep(j):
            def run(job, t):
                o = []
                for tt in range(2):
                    b = job.banks[tt]
                    o.append(p.op(AC, lambda e, b=b, tt=tt: e.activation(pu[:, tt, :], b[:, :], ACT.Copy), t, R.get("pu_free"), R["x0T"]))
                done(job, o)
                yield 1
                for g in range(2):
                    gg = 2 * j + g
                    ps, fr = yield from take(misc)
                    for ct in range(2):
                        for st in range(2):
                            f = lambda e, ct=ct, st=st, g=g, gg=gg, ps=ps: e.matmul(
                                ps[:, ct * 256:ct * 256 + 256], pu[:, st, g * 256 + ct * 128:g * 256 + ct * 128 + 128],
                                pm[:, st, gg, :], start=(st == 0), stop=(st == 1))
                            u = p.op(PE, f, fr, o, R["pm"])
                    R["pu_free"] = u
                    yield 1
                    tm, ftm = yield from take(tmp)
                    v = p.op(AC, lambda e, tm=tm, ps=ps: e.activation(tm[:, :], ps[:, :], ACT.Copy), u, ftm)
                    misc.put(ps, v)
                    yield 1
                    ps, fr = yield from take(misc)
                    for dt in range(2):
                        for ct in range(2):
                            f = lambda e, ct=ct, dt=dt, gg=gg, ps=ps, tm=tm: e.matmul(
                                ps[:, dt * 256:dt * 256 + 256], pw[:, gg, ct, dt * 128:dt * 128 + 128],
                                tm[:, ct * 256:ct * 256 + 256], start=(ct == 0), stop=(ct == 1))
                            u = p.op(PE, f, fr, v, R["pw"])
                    yield 1
                    tn, ftn = yield from take(tmp)
                    for dt in range(2):
                        k = PS0 + 2 * gg + dt
                        w = p.op(AC, lambda e, dt=dt, k=k, ps=ps, tn=tn: e.activation(
                            tn[:, dt * 256:dt * 256 + 256], ps[:, dt * 256:dt * 256 + 256], ACT.Copy, scale=vbt[:, k:k + 1]), u, ftn, R["vbt"])
                    misc.put(ps, w)
                    tmp.put(tm, u)
                    z = split(tn[:, :].rearrange("p (k t) -> p k t", k=2), w, OP1.hi[:, 2 * gg:2 * gg + 2, :], OP1.lo[:, 2 * gg:2 * gg + 2, :])
                    tmp.put(tn, z)
                    OP1.ready[2 * gg] = OP1.ready[2 * gg + 1] = z
                    R[f"pool{gg}"] = u
                    yield 1
            return run

        def conv_u(job, t):
            o = []
            for b in range(2):
                s = job.banks[b][:, :].rearrange("p (k t) -> p k t", k=2)
                o.append(p.op(AC, lambda e, b=b, s=s: e.activation(cu[:, 2 * b:2 * b + 2, :], s, ACT.Copy), t, R.get("cu_free")))
            R["cu"] = o
            done(job, o)
            return
            yield

        def conv_c(blk):
            def run(job, t):
                if blk == 0:
                    R["cz0"] = p.op(DV, lambda e: e.memset(cz[:, :, 0:2], 0.0))
                o = []
                for b in range(2):
                    s = job.banks[b][:, :].rearrange("p (k t) -> p k t", k=2)
                    o.append(p.op(DV, lambda e, b=b, s=s: e.tensor_tensor(cz[:, 2 * b:2 * b + 2, 2:258], s, cu[:, 2 * b:2 * b + 2, :], ALU.mult), t, R["cu"], R.get("cz_free")))
                done(job, o)
                yield 1
                for c in range(4):
                    ct = 4 * blk + c
                    w = lambda k, ct=ct: vbt[:, CW0 + 8 * k + ct:CW0 + 8 * k + ct + 1]
                    v = p.op(DV, lambda e, c=c, w=w: e.tensor_scalar(cu[:, c, :], cz[:, c, 0:256], w(0), None, ALU.mult), o, R["cz0"], R["vbt"])
                    for k in (1, 2):
                        v = p.op(DV, lambda e, c=c, w=w, k=k: e.scalar_tensor_tensor(cu[:, c, :], cz[:, c, k:k + 256], w(k), cu[:, c, :], ALU.mult, ALU.add), v)
                    yield 1
                R[f"cy{blk}"] = v
                R["cz_free"] = v
            return run

        def conv_b(blk):
            def run(job, t):
                yield from have(f"cy{blk}")
                o = []
                for b in range(2):
                    tm, ftm = yield from take(tmp)
                    s = job.banks[b][:, :].rearrange("p (k t) -> p k t", k=2)
                    d = tm[:, :].rearrange("p (k t) -> p k t", k=2)
                    u = p.op(DV, lambda e, b=b, s=s, d=d: e.tensor_tensor(d, s, cu[:, 2 * b:2 * b + 2, :], ALU.mult), t, R[f"cy{blk}"], ftm)
                    o.append(u)
                    k = 8 + 4 * blk + 2 * b
                    z = split(d, u, OP1.hi[:, k:k + 2, :], OP1.lo[:, k:k + 2, :])
                    tmp.put(tm, z)
                    OP1.ready[k] = OP1.ready[k + 1] = z
                R["cu_free"] = u
                done(job, o)
            return run

        def attn1():
            yield from have("pool3", "erow_w")
            load("flip", flip[:, :], a["k_flip"], R["erow_m"])
            bts = []
            for i in range(4):
                tm, ftm = yield from take(tmp)
                load(f"bt{i}", tm[:, :].rearrange("p (h s) -> p h s", h=2), bass.AP(scratch_e.tensor, 768 * i, [[1, 128], [384, 2], [1, 256]]), R["erow_w"], ftm)
                ps, fr = yield from take(misc)
                t = p.op(PE, lambda e, ps=ps, tm=tm: e.matmul(ps[:, :], flip[:, :], tm[:, :], start=True, stop=True), fr, R["flip"], R[f"bt{i}"])
                tmp.put(tm, t)
                v = p.op(AC, lambda e, ps=ps, i=i: e.activation(bt[:, 2 * i:2 * i + 2, :], ps[:, :].rearrange("p (h s) -> p h s", h=2), ACT.Copy), t, R["pool3"])
                misc.put(ps, v)
                bts.append(v)
                yield 2
            R["bt"] = bts
            yield from have("mk", "q1", "q0", "x0T")
            for h in range(8):
                ps, fr = yield from take(misc)
                g = h // 4
                for tt in range(2):
                    o = (0, 128, 384)
                    nk = 128 * (tt + 1)
                    f = lambda e, tt=tt, nk=nk, ps=ps, g=g, h=h, o=o: e.matmul(
                        ps[:, o[tt]:o[tt + 1]], qb[:, h, tt * 128:tt * 128 + 128], kt1[:, g, 0:nk], start=True, stop=True)
                    t = p.op(PE, f, fr, R["q0"], R["q1"], R["k1"])
                yield 1
                tm, ftm = yield from take(tmp)
                st = col(8)
                r0 = []
                for tt in range(2):
                    nk = 128 * (tt + 1)
                    L = tm[:, o[tt]:o[tt + 1]]
                    bb = bt[:, h, 128 * (1 - tt):256]
                    v = p.op(DV, lambda e, L=L, bb=bb, ps=ps, tt=tt, o=o: e.scalar_tensor_tensor(
                        L, ps[:, o[tt]:o[tt + 1]], ATT_SCALE, bb, ALU.mult, ALU.add), t, ftm, R["bt"])
                    r0.append(v)
                misc.put(ps, r0)
                for tt in range(2):
                    nk = 128 * (tt + 1)
                    L = tm[:, o[tt]:o[tt + 1]]
                    v = p.op(DV, lambda e, L=L, tt=tt, nk=nk, st=st: e.tensor_tensor_reduce(
                        L, L, mk[:, tt, 0:nk], 1.0, -3e38, ALU.add, ALU.max, st[:, tt:tt + 1]), r0, R["mk"])
                v = p.op(DV, lambda e, st=st: e.tensor_scalar(st[:, 2:4], st[:, 0:2], -1.0, None, ALU.mult), v)
                for tt in range(2):
                    L = tm[:, o[tt]:o[tt + 1]]
                    u = p.op(AC, lambda e, L=L, tt=tt, st=st: e.activation(
                        L, L, ACT.Exp, bias=st[:, 2 + tt:3 + tt], accum_out=st[:, 4 + tt:5 + tt]), v)
                yield 1
                v = p.op(DV, lambda e, st=st: e.reciprocal(st[:, 6:8], st[:, 4:6]), u)
                for tt in range(2):
                    L = tm[:, o[tt]:o[tt + 1]]
                    w = p.op(DV, lambda e, L=L, tt=tt, st=st: e.tensor_scalar(L, L, st[:, 6 + tt:7 + tt], None, ALU.mult), v, u)
                yield 1
                ps, fr = yield from take(misc)
                for i in range(3):
                    f = lambda e, i=i, ps=ps, tm=tm: e.transpose(ps[:, i * 128:i * 128 + 128], tm[:, (0, 128, 256)[i]:(0, 128, 256)[i] + 128], ident[:, :])
                    t = p.op(PE, f, fr, w)
                yield 1
                tn, ftn = yield from take(tmp)
                u = p.op(AC, lambda e, ps=ps, tn=tn: e.activation(tn[:, 0:384], ps[:, 0:384], ACT.Copy), t, ftn)
                misc.put(ps, u)
                tmp.put(tm, t)
                yield 1
                ps, fr = yield from take(misc)
                f = lambda e, ps=ps, tn=tn, g=g: e.matmul(ps[:, 0:256], v1[:, 0, g * 128:g * 128 + 128], tn[:, 0:256], start=True, stop=False)
                p.quiet(PE, f, fr, u, R["v1"])
                f = lambda e, ps=ps, tn=tn, g=g: e.matmul(ps[:, 128:256], v1[:, 1, g * 128:g * 128 + 128], tn[:, 256:384], start=False, stop=True)
                t = p.op(PE, f)
                tmp.put(tn, t)
                yield 1
                z = split(ps[:, 0:256], t, YA.hi[:, h, :], YA.lo[:, h, :], R["x0T"])
                misc.put(ps, z)
                YA.ready[h] = z
                yield 1
            R["attn1"] = z

        gate_tok = {}

        def gate_ep(n, c):
            def run(job, t):
                g = gt[(4 * n + c) % 2]
                fr = R.get(f"gtfree{(4 * n + c) % 2}")
                for m in range(4):
                    k = 64 + 16 * n + 4 * c + m
                    u = p.op(AC, lambda e, m=m, k=k: e.activation(
                        g[:, m, :], job.banks[m // 2][:, 256 * (m % 2):256 * (m % 2) + 256], ACT.Sigmoid, bias=vat[:, k:k + 1]),
                        t, R["vat"], fr, R["cy1"])
                gate_tok[n, c] = u
                done(job, u)
                return
                yield
            return run

        def branch_ep(n, c):
            def run(job, t):
                i = (4 * n + c) % 2
                g = gt[i]
                o = []
                for b in range(2):
                    s = job.banks[b][:, :].rearrange("p (k t) -> p k t", k=2)
                    m = mx[:, 4 * c + 2 * b:4 * c + 2 * b + 2, :]
                    gg = g[:, 2 * b:2 * b + 2, :]
                    if n == 0:
                        u = p.op(DV, lambda e, s=s, m=m, gg=gg: e.tensor_tensor(m, s, gg, ALU.mult), t, gate_tok[n, c], R["cu_free"], R["pool3"])
                        o.append(u)
                        continue
                    u = p.op(DV, lambda e, s=s, gg=gg: e.tensor_tensor(gg, s, gg, ALU.mult), t, gate_tok[n, c])
                    o.append(u)
                    v = p.op(DV, lambda e, m=m, gg=gg: e.tensor_tensor(m, m, gg, ALU.add), u, R[f"mx{c}"])
                    if n == 2:
                        k = 4 * c + 2 * b
                        z = split(m, v, OP1.hi[:, k:k + 2, :], OP1.lo[:, k:k + 2, :], OP1.read)
                        OP1.ready[k] = OP1.ready[k + 1] = z
                R[f"mx{c}"] = u if n == 0 else v
                R[f"gtfree{i}"] = R[f"mx{c}"]
                done(job, o)
                if (n, c) == (2, 3):
                    R["branches"] = [z]
                return
                yield
            return run

        def wout_ep(c):
            def run(job, t):
                if c == 0:
                    R["ssq"] = [None, None]
                ss = ss_t[0]
                o = []
                for tt in range(2):
                    tm, ftm = yield from take(tmp)
                    b = job.banks[tt]
                    u = p.op(AC, lambda e, b=b, tt=tt, tm=tm: e.activation(tm[:, :], b[:, :], ACT.Square, accum_out=ss[:, tt, c:c + 1]), t, ftm)
                    tmp.put(tm, u)
                    v = p.op(DV, lambda e, b=b, tt=tt: e.tensor_tensor(macc[:, tt, 512 * c:512 * c + 512], b[:, :], g1b[:, 512 * c:512 * c + 512], ALU.mult), u, R["g1b"])
                    o.append(v)
                done(job, o)
                if c == 3:
                    R["wout"] = v
                    start(after_mix())
            return run

        def after_mix():
            ss = ss_t[0]
            xs = []
            for tt in range(2):
                s = col()
                t = p.op(DV, lambda e, tt=tt, s=s: e.tensor_reduce(s[:, 0:1], ss[:, tt, 0:4], AX, ALU.add), R["wout"])
                t = rstd(s[:, 1:2], s[:, 0:1], t)
                xs.append(p.op(DV, lambda e, tt=tt, s=s: e.scalar_tensor_tensor(
                    X[:, tt, :], macc[:, tt, :], s[:, 1:2], X[:, tt, :], ALU.mult, ALU.add), t, R["xr"]))
            xn = norm_rows(X, macc, junk1[:, :], xs)
            yield from to_operand(macc, xn, lambda kt: vat[:, 32 + kt:33 + kt], None, OP0, last="x1T")
            ld = load("ctx", macc[:, :, :], a["ctx_2"].rearrange("b (t p) n -> p (b t) n", p=128), R["x1T"])
            yield from have("acol")
            cn = norm_rows(macc, macc, a_junk(), [ld] * 2, R["acol"])
            yield from to_operand(macc, cn, lambda kt: acol[:, kt, 1:2], lambda kt: abt[:, kt, 1:2], HC, R["acol"], R["x1T"], last="ctxT")

        def a_junk():
            return junk4[:, :]

        def up_ep(blk, c):
            def run(job, t):
                for b in range(2):
                    tm, ftm = yield from take(tmp)
                    k = 4 * c + 2 * b
                    bk = job.banks[b]
                    u = p.op(AC, lambda e, bk=bk, tm=tm: e.activation(tm[:, :], bk[:, :], ACT.Relu), t, ftm)
                    if b == 0:
                        u0 = u
                    v = p.op(DV, lambda e, tm=tm: e.tensor_tensor(tm[:, :], tm[:, :], tm[:, :], ALU.mult), u)
                    z = split(tm[:, :].rearrange("p (k t) -> p k t", k=2), v, OP1.hi[:, k:k + 2, :], OP1.lo[:, k:k + 2, :], OP1.read)
                    tmp.put(tm, z)
                    OP1.ready[k] = OP1.ready[k + 1] = z
                done(job, u0, u)
            return run

        def down_ep(blk, c):
            def run(job, t):
                o = []
                for tt in range(2):
                    b = job.banks[tt]
                    m = macc[:, tt, 512 * c:512 * c + 512]
                    if blk == 0:
                        u = p.op(AC, lambda e, b=b, m=m: e.activation(m, b[:, :], ACT.Copy), t, R["ctxT"])
                    else:
                        u = p.op(DV, lambda e, b=b, m=m: e.tensor_tensor(m, b[:, :], m, ALU.add), t, R[f"mlp{c}"])
                    o.append(u)
                    if blk == 3:
                        tm, ftm = yield from take(tmp)
                        v = p.op(AC, lambda e, m=m, tt=tt, tm=tm: e.activation(tm[:, :], m, ACT.Square, accum_out=ss_t[1][:, tt, c:c + 1]), u, ftm)
                        tmp.put(tm, v)
                        R["ssq"] = v
                R[f"mlp{c}"] = o
                done(job, o)
                if (blk, c) == (3, 3):
                    start(after_mlp(o))
            return run

        def after_mlp(o):
            ss = ss_t[1]
            load("g3b", g3b[:, :], a["norm_gains"][0, 3:4, :].partition_broadcast(128).rearrange("p a n -> p (a n)"), OP1.read)
            xs = []
            for tt in range(2):
                s = col()
                t = p.op(DV, lambda e, tt=tt, s=s: e.tensor_reduce(s[:, 0:1], ss[:, tt, 0:4], AX, ALU.add), R["ssq"], o)
                t = rstd(s[:, 1:2], s[:, 0:1], t)
                t = p.op(DV, lambda e, tt=tt, s=s: e.scalar_tensor_tensor(
                    macc[:, tt, :], macc[:, tt, :], s[:, 1:2], g3b[:, :], ALU.mult, ALU.mult), t, R["g3b"], R["mlp0"], R["mlp1"], R["mlp2"])
                xs.append(p.op(DV, lambda e, tt=tt: e.tensor_tensor(X[:, tt, :], X[:, tt, :], macc[:, tt, :], ALU.add), t))
            R["xw"] = p.dma(PO, p.new_sem("d_xw"), scratch_x.rearrange("(t p) n -> p t n", p=128), X[:, :, :], *xs)
            xn = norm_rows(X, macc, junk3[:, :], xs)
            R["x2n"] = xn
            yield from to_operand(macc, xn, lambda kt: acol[:, kt, 0:1], lambda kt: abt[:, kt, 0:1], OP0, R["acol"], last="x2T")

        def qk_ep(kind, j):
            def run(job, t):
                g = gqk[:, 0 if kind == "q" else 1, :]
                rope = kind != "kc"
                dst = {"q": qt, "k": ktx, "kc": ktc}[kind]
                fin, outs = [], []
                for tt in range(2):
                    b = job.banks[tt]
                    t1, f1 = yield from take(tmp)
                    s = col(8)
                    u = p.op(AC, lambda e, b=b, t1=t1: e.activation(t1[:, :], b[:, :], ACT.Square), t, f1)
                    v = p.op(DV, lambda e, t1=t1, s=s: e.tensor_reduce(s[:, 0:4], t1[:, :].rearrange("p (h d) -> p h d", h=4), AX, ALU.add), u)
                    v = rstd(s[:, 4:8], s[:, 0:4], v, 128)
                    for h in range(4):
                        w = p.op(DV, lambda e, h=h, b=b, t1=t1, s=s: e.scalar_tensor_tensor(
                            t1[:, 128 * h:128 * h + 128], b[:, 128 * h:128 * h + 128], s[:, 4 + h:5 + h], g, ALU.mult, ALU.mult), v, R["gq"], R["gk"])
                    fin.append(w)
                    if rope:
                        t2, f2 = yield from take(tmp)
                        sv = t1[:, :].rearrange("p (a h f) -> p a h f", h=2, f=32)
                        dv = t2[:, :].rearrange("p (a h f) -> p a h f", h=2, f=32)
                        rv = rst[:, tt, :].rearrange("p (a h f) -> p a h f", h=2, f=32)
                        y1 = p.op(DV, lambda e, sv=sv, dv=dv, rv=rv: e.tensor_tensor(dv[:, :, 0, :], sv[:, :, 1, :], rv[:, :, 0, :], ALU.mult), w, f2, R["rope"])
                        y2 = p.op(DV, lambda e, sv=sv, dv=dv, rv=rv: e.tensor_tensor(dv[:, :, 1, :], sv[:, :, 0, :], rv[:, :, 1, :], ALU.mult), w)
                        y3 = p.op(DV, lambda e, t1=t1, tt=tt: e.tensor_tensor(t1[:, :], t1[:, :], rct[:, tt, :], ALU.mult), y1, y2)
                        w = p.op(DV, lambda e, t1=t1, t2=t2: e.tensor_tensor(t1[:, :], t1[:, :], t2[:, :], ALU.add), y3)
                        tmp.put(t2, w)
                    outs.append((t1, w))
                done(job, fin)
                yield 1
                for tt in range(2):
                    t1, w = outs[tt]
                    ps, fr = yield from take(misc)
                    for h in range(4):
                        f = lambda e, h=h, ps=ps, t1=t1: e.transpose(ps[:, 128 * h:128 * h + 128], t1[:, 128 * h:128 * h + 128], ident[:, :])
                        u = p.op(PE, f, fr, w)
                    tmp.put(t1, u)
                    h0 = 4 * j
                    v = p.op(AC, lambda e, ps=ps, tt=tt, h0=h0: e.activation(
                        dst[:, h0:h0 + 4, 128 * tt:128 * tt + 128], ps[:, :].rearrange("p (h t) -> p h t", h=4), ACT.Copy), u, R.get("x2T"), R["branches"])
                    misc.put(ps, v)
                    R[f"{kind}t{j}"] = v
                    yield 1
            return run

        def v_ep(dst, name, *war):
            def run(job, t):
                o = []
                for tt in range(2):
                    b = job.banks[tt]
                    o.append(p.op(AC, lambda e, b=b, tt=tt: e.activation(dst[:, tt, :], b[:, :], ACT.Copy), t, [R[w] for w in war]))
                R[name] = o
                done(job, o)
                return
                yield
            return run

        def silu_ep(k0, name):
            def run(job, t):
                o = []
                for b in range(2):
                    s = job.banks[b][:, :].rearrange("p (k t) -> p k t", k=2)
                    d = zs[:, k0 + 2 * b:k0 + 2 * b + 2, :]
                    u = p.op(AC, lambda e, s=s, d=d: e.activation(d, s, ACT.Sigmoid), t, R["xw"], R["x2n"])
                    o.append(p.op(DV, lambda e, s=s, d=d: e.tensor_tensor(d, s, d, ALU.mult), u))
                R[name] = o
                done(job, o)
                return
                yield
            return run

        def fourier():
            yield from have("ub", "zb")
            for g in range(4):
                ps, fr = yield from take(misc)
                for tt in range(2):
                    f = lambda e, tt=tt, g=g, ps=ps: e.matmul(ps[:, :], ub[:, tt, 128 * g:128 * g + 128], cst[:, tt, :], start=(tt == 0), stop=(tt == 1))
                    t = p.op(PE, f, fr, R["ub"], R["fft"])
                yield 1
                tm, ftm = yield from take(tmp)
                u = p.op(AC, lambda e, ps=ps, tm=tm: e.activation(tm[:, :], ps[:, :], ACT.Copy), t, ftm)
                misc.put(ps, u)
                yield 1
                ps, fr = yield from take(misc)
                for i in range(2):
                    f = lambda e, i=i, ps=ps, tm=tm: e.matmul(ps[:, 0:256], cdt[:, i, :], tm[:, 256 * i:256 * i + 256], start=(i == 0), stop=(i == 1))
                    t = p.op(PE, f, fr, u)
                tmp.put(tm, t)
                yield 1
                tm, ftm = yield from take(tmp)
                v = p.op(DV, lambda e, ps=ps, tm=tm, g=g: e.tensor_tensor(tm[:, 0:256], ps[:, 0:256], zs[:, 12 + g, :], ALU.mult), t, ftm, R["zb"])
                misc.put(ps, v)
                z = split(tm[:, 0:256], v, OP1.hi[:, 12 + g, :], OP1.lo[:, 12 + g, :], OP1.read, R["x2n"])
                tmp.put(tm, z)
                OP1.ready[12 + g] = z
                yield 1
            R["fourier"] = [z, t]

        def attn2(hs):
            yield from have("kt0", "vx", "kct0", "vc")
            for h in hs:
                yield from have(f"qt{h // 4}")
                kv = h // 3
                pts = []
                for tt in range(2):
                    ps, fr = yield from take(misc)
                    for i, kk in enumerate((ktx, ktc)):
                        f = lambda e, i=i, kk=kk, ps=ps, tt=tt, h=h, kv=kv: e.matmul(
                            ps[:, 256 * i:256 * i + 256], qt[:, h, 128 * tt:128 * tt + 128], kk[:, kv, :], start=True, stop=True)
                        t = p.op(PE, f, fr, R[f"qt{h // 4}"], R["kt0"], R["kct0"])
                    yield 1
                    st = col(4)
                    v = p.op(DV, lambda e, ps=ps, st=st: e.tensor_reduce(st[:, 0:1], ps[:, :], AX, ALU.max), t)
                    v = p.op(DV, lambda e, st=st: e.tensor_scalar(st[:, 1:2], st[:, 0:1], -ATT_SCALE, None, ALU.mult), v)
                    tm, ftm = yield from take(tmp)
                    u = p.op(AC, lambda e, ps=ps, st=st, tm=tm: e.activation(
                        tm[:, :], ps[:, :], ACT.Exp, bias=st[:, 1:2], scale=ATT_SCALE, accum_out=st[:, 2:3]), v, ftm)
                    misc.put(ps, u)
                    yield 1
                    v = p.op(DV, lambda e, st=st: e.reciprocal(st[:, 3:4], st[:, 2:3]), u)
                    w = p.op(DV, lambda e, st=st, tm=tm: e.tensor_scalar(tm[:, :], tm[:, :], st[:, 3:4], None, ALU.mult), v)
                    ps, fr = yield from take(misc)
                    for i in range(4):
                        f = lambda e, i=i, ps=ps, tm=tm: e.transpose(ps[:, 128 * i:128 * i + 128], tm[:, 128 * i:128 * i + 128], ident[:, :])
                        t = p.op(PE, f, fr, w)
                    yield 1
                    u = p.op(AC, lambda e, ps=ps, tm=tm: e.activation(tm[:, :], ps[:, :], ACT.Copy), t)
                    misc.put(ps, u)
                    pts.append((tm, u))
                ps, fr = yield from take(misc)
                for tt in range(2):
                    tm, u = pts[tt]
                    for st_ in range(4):
                        vv = vx if st_ < 2 else vc
                        f = lambda e, st_=st_, tt=tt, tm=tm, vv=vv, ps=ps, kv=kv: e.matmul(
                            ps[:, 128 * tt:128 * tt + 128], vv[:, st_ % 2, 128 * kv:128 * kv + 128], tm[:, 128 * st_:128 * st_ + 128],
                            start=(st_ == 0), stop=(st_ == 3))
                        t = p.op(PE, f, fr, u, R["vx"], R["vc"])
                    tmp.put(tm, t)
                yield from have(f"za{h // 4}")
                yield 1
                tm, ftm = yield from take(tmp)
                v = p.op(DV, lambda e, ps=ps, tm=tm, h=h: e.tensor_tensor(tm[:, 0:256], ps[:, 0:256], zs[:, h, :], ALU.mult), t, ftm, R[f"za{h // 4}"])
                misc.put(ps, v)
                z = split(tm[:, 0:256], v, OP1.hi[:, h, :], OP1.lo[:, h, :], OP1.read, R["x2n"])
                tmp.put(tm, z)
                OP1.ready[h] = z
            R[f"attn2{hs[0] % 2}"] = [t, z]

        def after_attn2():
            yield from have("attn20", "attn21", "fourier")
            R["attn2"] = [R["attn20"], R["attn21"]]
            z = R["attn2"]
            load("xr2", X2[:, :, :], scratch_x.rearrange("(t p) n -> p t n", p=128), z, R["fourier"], R["xw"])

        def gate2_ep(buf, c, name):
            def run(job, t):
                yield from have("fourier")
                for m in range(4):
                    u = p.op(AC, lambda e, m=m: e.activation(
                        buf[c % 2][:, m, :], job.banks[m // 2][:, 256 * (m % 2):256 * (m % 2) + 256], ACT.Sigmoid),
                        t, R.get(f"{name}free{c % 2}"), R["fourier"], R["x2n"])
                R[f"{name}{c}"] = u
                done(job, u)
                return
                yield
            return run

        def pb_wait(c):
            def run(j, t):
                yield from have(f"gb{c}")
                o = []
                for b in range(2):
                    s = j.banks[b][:, :].rearrange("p (k t) -> p k t", k=2)
                    g = gb[c % 2][:, 2 * b:2 * b + 2, :]
                    o.append(p.op(DV, lambda e, s=s, g=g: e.tensor_tensor(g, s, g, ALU.mult), t, R[f"gb{c}"]))
                R[f"pb{c}"] = o
                done(j, o)
            return run

        def pa_wait(c):
            def run(j, t):
                yield from have(f"ga{c}", f"pb{c}", "attn2")
                o = []
                for b in range(2):
                    s = j.banks[b][:, :].rearrange("p (k t) -> p k t", k=2)
                    g = ga[c % 2][:, 2 * b:2 * b + 2, :]
                    m = gb[c % 2][:, 2 * b:2 * b + 2, :]
                    u = p.op(DV, lambda e, s=s, g=g: e.tensor_tensor(g, s, g, ALU.mult), t, R[f"ga{c}"])
                    o.append(u)
                    v = p.op(DV, lambda e, m=m, g=g: e.tensor_tensor(g, m, g, ALU.add), u, R[f"pb{c}"])
                    k = 4 * c + 2 * b
                    z = split(g, v, MG.hi[:, k:k + 2, :], MG.lo[:, k:k + 2, :], R["attn2"], R["fourier"])
                    MG.ready[k] = MG.ready[k + 1] = z
                R[f"gafree{c % 2}"] = R[f"gbfree{c % 2}"] = z
                done(j, o)
            return run

        def out2_ep(c):
            def run(job, t):
                o = []
                if c == 0:
                    load("fgb", fgb[:, :], a["final_g_2"].partition_broadcast(128), OP1.read)
                for tt in range(2):
                    tm, ftm = yield from take(tmp)
                    b = job.banks[tt]
                    u = p.op(DV, lambda e, b=b, tm=tm: e.tensor_tensor(tm[:, :], b[:, :], gbc[:, 512 * c:512 * c + 512], ALU.mult), t, ftm, R[f"ada{8 + c}"])
                    o.append(u)
                    v = p.op(DV, lambda e, tm=tm, tt=tt: e.tensor_tensor(X2[:, tt, 512 * c:512 * c + 512], X2[:, tt, 512 * c:512 * c + 512], tm[:, :], ALU.add), u, R["xr2"])
                    w = p.op(AC, lambda e, tt=tt, tm=tm: e.activation(tm[:, :], X2[:, tt, 512 * c:512 * c + 512], ACT.Square, accum_out=ss_t[2][:, tt, c:c + 1]), v)
                    tmp.put(tm, w)
                    R["ss2"] = w
                done(job, o)
                if c == 3:
                    outs = []
                    for tt in range(2):
                        s = col()
                        t = p.op(DV, lambda e, tt=tt, s=s: e.tensor_reduce(s[:, 0:1], ss_t[2][:, tt, 0:4], AX, ALU.add), w)
                        t = rstd(s[:, 1:2], s[:, 0:1], t)
                        for hf in range(2):
                            sl = slice(1024 * hf, 1024 * hf + 1024)
                            t2 = p.op(DV, lambda e, tt=tt, s=s, sl=sl: e.scalar_tensor_tensor(
                                X2[:, tt, sl], X2[:, tt, sl], s[:, 1:2], fgb[:, sl], ALU.mult, ALU.mult), t, R["fgb"])
                            outs.append(p.dma(SP, p.new_sem(f"d_out{tt}{hf}"), out[0].rearrange("(t p) n -> p t n", p=128)[:, tt, sl], X2[:, tt, sl], t2))
                    p.wait(SP, *outs)
            return run

        ss_t = [ss_all[:, i, :, :] for i in range(3)]

        w_in, w_in2 = a["w_in"][0], a["w_in_2"][0]
        wbr, wg = a["w_branch"][0], a["w_gate"][0]
        p.new_sem("d_a5")
        jobs = []

        def J(mode, op, w, cols, ep, nkt=16, kt0=0, wk0=0, need=()):
            wv = w.rearrange("(k p) n -> p k n", p=128)[:, wk0:wk0 + nkt, :]
            return Job(mode, op, wv, kt0, nkt, cols, ep, need)

        C4 = Operand(c4, c4)

        def A(j):
            return J("ada", C4, a["w_ada_2"][0], [(512 * j, 512)], ada(j), need=("c4",))

        def W(op, w, c0, ep, **k):
            return J("W", op, w, [(c0, 512)], ep, **k)

        def T(op, w, c0, ep, n=512, **k):
            return J("T", op, w, [(c0, n)], ep, **k)

        sideq = []

        def chunks(job):
            return [(job, k, min(KC, job.nkt - k)) for k in range(0, job.nkt, KC)]

        seq = []

        def add(*js):
            for j in js:
                seq.extend(chunks(j))

        def merge(main_jobs, side_jobs, every):
            m = [c for j in main_jobs for c in chunks(j)]
            s = [c for j in side_jobs for c in chunks(j)]
            for i, c in enumerate(m):
                seq.append(c)
                if i % every == every - 1 and s:
                    seq.append(s.pop(0))
            seq.extend(s)

        add(A(0), A(1))
        ph1 = [
            W(OP0, w_in, 5632, ev_copy(qb, "qi0", "x0T")),
            W(OP0, w_in, 6144, ev_copy(qb[:, 4:8, :], "qi1")),
            J("W", OP0, w_in, [(5120, 256), (6656, 64), (6656, 64)], ep_kk),
            J("T", OP0, w_in, [(5376, 256), (6720, 16)], ep_vw),
            T(OP0, w_in, 0, pool_ep(0)),
            T(OP0, w_in, 512, pool_ep(1)),
        ]
        for blk in range(2):
            ph1 += [W(OP0, w_in, 1024 + 512 * blk, conv_u), W(OP0, w_in, 2048 + 512 * blk, conv_c(blk)),
                    W(OP0, w_in, 3072 + 512 * blk, conv_b(blk))]
        ph1 += [W(OP0, w_in, 4096, ev_copy(qb, "q0", "qi_done")), W(OP0, w_in, 4608, ev_copy(qb[:, 4:8, :], "q1", "qi_done"))]
        for n, op, k0 in ((0, OP1, 0), (1, OP1, 8), (2, YA, 0)):
            for c in range(4):
                ph1 += [W(OP0, wg, 2048 * n + 512 * c, gate_ep(n, c)),
                        W(op, wbr[n], 512 * c, branch_ep(n, c), nkt=8, kt0=k0)]
        merge(ph1, [A(j) for j in range(2, 7)], 6)
        add(*[T(OP1, a["w_out"][0], 512 * c, wout_ep(c)) for c in range(4)])
        add(A(7))
        mid = []
        for blk in range(4):
            mid += [W(OP0, a["w_up"][0], 2048 * blk + 512 * c, up_ep(blk, c)) for c in range(4)]
            mid += [T(OP1, a["w_down"][0], 512 * c, down_ep(blk, c), wk0=16 * blk) for c in range(4)]
        add(*mid)
        add(T(HC, w_in2, 1536, qk_ep("kc", 0)), T(HC, w_in2, 2048, v_ep(vc, "vc", "branches")))
        add(T(OP0, w_in2, 1536, qk_ep("k", 0)),
            T(OP0, w_in2, 2048, v_ep(vx, "vx", "x2T")),
            T(OP0, w_in2, 0, qk_ep("q", 0)),
            W(OP0, w_in2, 2560, silu_ep(0, "za0")),
            T(OP0, w_in2, 512, qk_ep("q", 1)),
            T(OP0, w_in2, 4096, v_ep(ub, "ub", "x2T")),
            W(OP0, w_in2, 4608, silu_ep(12, "zb")),
            T(OP0, w_in2, 1024, qk_ep("q", 2)),
            W(OP0, w_in2, 3072, silu_ep(4, "za1")),
            W(OP0, w_in2, 3584, silu_ep(8, "za2")))
        def g2(c):
            return [W(OP0, w_in2, 5120 + 512 * c, gate2_ep(ga, c, "ga")),
                    W(OP0, w_in2, 7168 + 512 * c, gate2_ep(gb, c, "gb")),
                    W(OP1, a["w_proj_b_2"][0], 512 * c, pb_wait(c), nkt=4, kt0=12)]

        def pa(c):
            return [W(OP1, a["w_proj_a_2"][0], 512 * c, pa_wait(c), nkt=12, kt0=0)]

        add(*g2(0), *g2(1))
        merge(pa(0) + pa(1) + g2(2) + pa(2) + g2(3) + pa(3), [A(j) for j in range(8, 12)], 2)
        add(*[T(MG, a["w_out_2"][0], 512 * c, out2_ep(c)) for c in range(4)])

        hooks = {}

        def at_job(job_name_chunk, fn):
            hooks.setdefault(job_name_chunk, []).append(fn)

        start(setup())
        start(bias_table())
        load("pm", pm[:, :, :, :], a["k_pm"].rearrange("p (s g t) -> p s g t", s=2, g=4))

        def late_loads():
            yield from have("x0T")
            load("pw", pw[:, :, :, :], a["pool_w"].rearrange("l g (c p) d -> p (l g) c d", p=128), R["x0T"])
            yield from have("branches")
            w = [R["branches"], R["attn1"]]
            load("xr", X[:, :, :], a["x"].rearrange("b (t p) n -> p (b t) n", p=128), *w)
            load("g1b", g1b[:, :], a["norm_gains"][0, 1:2, :].partition_broadcast(128).rearrange("p a n -> p (a n)"), *w)
            yield from have("vc")
            while HCjobs_read() is None:
                yield 1
            w = [HC.read]
            R["rope1"] = load("rope_c", rct[:, :, :], a["k_rc"].rearrange("p (t n) -> p t n", t=2), *w)
            R["rope2"] = load("rope_s", rst[:, :, :], a["k_rs"].rearrange("p (t n) -> p t n", t=2), *w)
            R["rope"] = [R["rope1"], R["rope2"]]
            f1 = load("cs", cst[:, :, :], a["k_cs"].rearrange("p (t n) -> p t n", t=2), *w)
            f2 = load("cd", cdt[:, :, :], a["k_cd"].rearrange("p (t n) -> p t n", t=2), *w)
            R["fft"] = [f1, f2]
            start(attn2(range(0, 12, 2)))
            start(attn2(range(1, 12, 2)))
            start(after_attn2())
            start(fourier())

        def HCjobs_read():
            return HC.read if R.get("vc") else None

        start(late_loads())
        start(attn1())
        junk4 = bg("junk4", [128, 2048], 40)

        n = len(seq)
        lo_tok, pe_tok = {}, {}
        state = {"dma": 0, "split": 0}

        def emit_dma(i):
            job, k, nk = seq[i]
            w = [lo_tok[i - NRAW]] if i >= NRAW else []
            sl = i % NRAW
            o = 0
            for c0, cn in job.cols:
                t = p.dma(SP, raw_sem[sl], raw[sl][:, 0:nk, o:o + cn], job.w[:, k:k + nk, c0:c0 + cn], *w)
                o += cn
            return t

        dma_tok = {}

        def emit_split(i):
            job, k, nk = seq[i]
            w = [pe_tok[i - NSPL]] if i >= NSPL else []
            r, h, l = raw[i % NRAW], whi[i % NSPL], wlo[i % NSPL]
            r, h, l = (x[:, 0:nk, 0:job.n] for x in (r, h, l))
            t = p.op(AC, lambda e: e.activation(h, r, ACT.Copy), dma_tok[i], *w)
            lo_tok[i] = p.op(DV, lambda e: e.tensor_tensor(l, r, h.bitcast(F32), ALU.subtract), t, dma_tok[i], *w)

        def emit_pe(i):
            job, k, nk = seq[i]
            if job.banks is None:
                pool = side if job.mode == "ada" else main
                until(lambda: pool.free, "banks")
                job.banks, job.fr = pool.free.pop(0)
                for x in job.need:
                    until(lambda: x in R, x)
                job.wait0 = [job.fr] + [R[x] for x in job.need]
            op = job.op
            if job.mode != "ada":
                for kk in range(k, k + nk):
                    until(lambda: job.kt0 + kk in op.ready, ("operand", i, kk))
                job.wait0 += [op.ready[job.kt0 + kk] for kk in range(k, k + nk)]
            w = job.wait0 + [lo_tok[i]]
            h, l = whi[i % NSPL], wlo[i % NSPL]
            last = None
            mms = []
            for kk in range(nk):
                kg = k + kk
                ka = job.kt0 + kg
                end = kg == job.nkt - 1
                if job.mode == "ada":
                    for m, ww in enumerate((h, l)):
                        mms.append((job.banks[:, :], op.hi[:, 4 * ka:4 * ka + 128], ww[:, kk, 0:512], kg == 0 and m == 0, end and m == 1))
                elif job.mode == "T":
                    for tt in range(2):
                        xh, xl = (x[:, ka, 128 * tt:128 * tt + 128] for x in (op.hi, op.lo))
                        o = job.banks[tt][:, 0:job.n]
                        mms.append((o, xh, h[:, kk, 0:job.n], kg == 0, False))
                        mms.append((o, xh, l[:, kk, 0:job.n], False, False))
                        mms.append((o, xl, h[:, kk, 0:job.n], False, end))
                else:
                    for m in range(job.n // 128):
                        o = job.banks[m // 2][:, 256 * (m % 2):256 * (m % 2) + 256]
                        wh, wl = (x[:, kk, 128 * m:128 * m + 128] for x in (h, l))
                        xh, xl = op.hi[:, ka, :], op.lo[:, ka, :]
                        mms.append((o, wh, xh, kg == 0 and m % 2 == 0, False))
                        mms.append((o, wh, xl, False, False))
                        mms.append((o, wl, xh, False, end))
            for q, (o, x, y, s, e_) in enumerate(mms):
                f = lambda e, o=o, x=x, y=y, s=s, e_=e_: e.matmul(o, x, y, start=s, stop=e_, skip_group_check=True)
                if q < len(mms) - 1:
                    p.quiet(PE, f, w)
                else:
                    last = p.op(PE, f, w)
            job.wait0 = []
            pe_tok[i] = last
            if k + nk == job.nkt:
                job.op.read = last
                start(job.epilogue(job, last))

        for i in range(-AHEAD, n):
            j = i + AHEAD
            for d in range(state["dma"], min(n, j + NRAW)):
                if d < NRAW or d - NRAW in lo_tok:
                    dma_tok[d] = emit_dma(d)
                    state["dma"] = d + 1
            if j < n:
                emit_split(j)
            if i >= 0:
                step()
                emit_pe(i)
        k = 0
        while tasks:
            step()
            k += 1
            assert k < 1000
        for e in (PE, AC, DV):
            p.wait(SP, (e, p.count[e]))

        block = ctx.enter_context(nc.Block())

        def flush(eng, name):
            for f in p.q[name]:
                f(eng)

        @block.sync
        def _(eng):
            flush(eng, SP)

        @block.gpsimd
        def _(eng):
            flush(eng, PO)

        @block.scalar
        def _(eng):
            flush(eng, AC)

        @block.vector
        def _(eng):
            flush(eng, DV)

        @block.tensor
        def _(eng):
            flush(eng, PE)


_INS = ["x", "norm_gains", "w_in", "pool_w", "pool_scale", "conv_w", "rel_bias", "w_branch", "w_gate", "b_gate",
        "w_out", "w_up", "w_down", "c_2", "ctx_2", "c_ctx_2", "w_ada_2", "b_ada_2", "norm_g_2", "w_in_2",
        "q_norm_g_2", "k_norm_g_2", "w_proj_a_2", "w_proj_b_2", "w_out_2", "final_g_2"]


def kernel(**inputs):
    import concourse.bacc as _bacc
    from concourse.bass_utils import run_bass_kernel_spmd as _run

    nc = _bacc.Bacc("TRN2", target_bir_lowering=False, num_devices=1)
    arrays, aps = {}, {}
    given = {n: np.ascontiguousarray(inputs[n]) for n in _INS}
    given.update(constants())
    for name, v in given.items():
        arrays[f"in_{name}"] = v
        aps[name] = nc.dram_tensor(f"in_{name}", v.shape, mybir.dt.from_np(v.dtype), kind="ExternalInput").ap()
    out = nc.dram_tensor("out_dram", (1, 256, D), F32, kind="ExternalOutput").ap()
    se = nc.dram_tensor("scratch_e", (8, 384), F32).ap()
    sx = nc.dram_tensor("scratch_x", (256, D), F32).ap()
    program(nc, aps, out, se, sx)
    r = _run(nc, [arrays], core_ids=[0])
    return r.results[0]["out_dram"]
```

```python
import math
from contextlib import ExitStack

import numpy as np

import concourse.bass as bass
from concourse import mybir
from concourse.alu_op_type import AluOpType as ALU

ACT = mybir.ActivationFunctionType
AX = mybir.AxisListType.X
F32 = mybir.dt.float32
F32R = mybir.dt.float32r

D = 2048
EPS = 1e-6
HID = 8192
KC = 2
NRAW = 5
NSPL = 4
AHEAD = 3
ATT_SCALE = 128 ** -0.5
BIG = 1e30
PE, AC, DV, PO, SP = "pe", "act", "dve", "pool", "sp"


def constants():
    t = np.arange(256)
    pm = np.zeros((256, 4, 256), np.float64)
    for g, w in enumerate((2, 4, 8, 16)):
        for i in t:
            lo = max(i + 1 - w, 0)
            pm[lo:i + 1, g, i] = 1.0 / (i + 1 - lo)
            pm[i, g, i] -= 1.0
    pm = pm.reshape(2, 128, 4 * 256).transpose(1, 0, 2).reshape(128, 2048)
    onehot = np.zeros((32, 384), np.float32)
    for j in range(384):
        d = 255 - j
        if d >= 0:
            b = d if d < 16 else min(16 + int(math.log(d / 16) / math.log(8) * 16), 31)
            onehot[b, j] = 1.0
    cm = np.where(t[None, :] <= t[:, None], 0.0, -BIG)
    cm = cm.reshape(2, 128, 256).transpose(1, 0, 2).reshape(128, 512)
    inv = np.float32(10000.0) ** (-np.arange(32, dtype=np.float32) / np.float32(32))
    ang = np.stack([(t // 64).astype(np.float32)[:, None] * inv, (t % 64).astype(np.float32)[:, None] * inv], 1)
    co, si = np.cos(ang.astype(np.float64)), np.sin(ang.astype(np.float64))
    rc = np.tile(np.stack([co, co], 2).reshape(256, 128), (1, 4))
    rs = np.tile(np.stack([-si, si], 2).reshape(256, 128), (1, 4))
    rc = rc.reshape(2, 128, 512).transpose(1, 0, 2).reshape(128, 1024)
    rs = rs.reshape(2, 128, 512).transpose(1, 0, 2).reshape(128, 1024)
    a = 2 * np.pi * (np.outer(t, t) % 256) / 256
    cs = np.concatenate([np.cos(a), np.sin(a)], 1).reshape(2, 128, 512).transpose(1, 0, 2).reshape(128, 1024)
    d = np.arange(128)
    b = 2 * np.pi * (np.outer(d, d) % 128) / 128
    cd = np.concatenate([np.cos(b), -np.sin(b)], 1) / math.sqrt(256 * 128)
    f = {"k_ident": np.eye(128), "k_flip": np.eye(128)[::-1], "k_pm": pm, "k_onehot": onehot, "k_cm": cm, "k_rc": rc, "k_rs": rs,
         "k_cs": cs, "k_cd": cd}
    return {n: np.ascontiguousarray(v, dtype=np.float32) for n, v in f.items()}


class Program:

    def __init__(self, nc, ctx):
        self.nc, self.ctx = nc, ctx
        self.q = {e: [] for e in (PE, AC, DV, PO, SP)}
        self.seen = {e: {} for e in self.q}
        self.count = {}
        self.sems = {}
        for e in (PE, AC, DV, PO):
            self.new_sem(e)

    def new_sem(self, name):
        self.sems[name] = self.ctx.enter_context(self.nc.semaphore("s_" + name))
        self.count[name] = 0
        return name

    def wait(self, eng, *tokens):
        for t in tokens:
            if t is None:
                continue
            if isinstance(t, list):
                self.wait(eng, *t)
                continue
            name, value = t
            if self.seen[eng].get(name, 0) < value:
                self.seen[eng][name] = value
                s = self.sems[name]
                self.q[eng].append(lambda e, s=s, v=value: e.wait_ge(s, v))

    def op(self, eng, fn, *tokens):
        self.wait(eng, *tokens)
        self.count[eng] += 1
        s = self.sems[eng]
        self.q[eng].append(lambda e: fn(e).then_inc(s, 1))
        return (eng, self.count[eng])

    def quiet(self, eng, fn, *tokens):
        self.wait(eng, *tokens)
        self.q[eng].append(fn)

    def dma(self, eng, sem, dst, src, *tokens):
        self.wait(eng, *tokens)
        self.count[sem] += 16
        s = self.sems[sem]
        self.q[eng].append(lambda e: e.dma_start(dst, src).then_inc(s, 16))
        return (sem, self.count[sem])


class Pool:

    def __init__(self, bufs):
        self.free = [(b, []) for b in bufs]

    def put(self, b, *tokens):
        self.free.append((b, list(tokens)))


class Operand:

    def __init__(self, hi, lo):
        self.hi, self.lo = hi, lo
        self.read = None
        self.ready = {}


class Job:
    def __init__(self, mode, op, w, kt0, nkt, cols, epilogue, need=(), gate=None):
        self.mode, self.op, self.w, self.kt0, self.nkt, self.cols = mode, op, w, kt0, nkt, cols
        self.epilogue, self.need = epilogue, need
        self.n = sum(c[1] for c in cols)
        self.banks = None


def program(nc, a, out, scratch_e, scratch_x):
    ctx = ExitStack()
    with ctx:
        ctx.enter_context(nc.allow_low_precision("float32 values are kept in two exact float32r parts"))
        p = Program(nc, ctx)
        base = nc.sbuf_base
        top = [(base + 63) // 64 * 64]

        def at(name, shape, off, dt=F32):
            return nc.alloc_sbuf_tensor_at(name, shape, dt, offset=off)

        def sb(name, shape, dt=F32):
            size = 4 * int(np.prod(shape[1:]))
            t = at(name, shape, top[0], dt)
            top[0] += (size + 31) // 32 * 32
            return t

        raw = [sb(f"raw{i}", [128, KC, 512]) for i in range(NRAW)]
        whi = [sb(f"whi{i}", [128, KC, 512], F32R) for i in range(NSPL)]
        wlo = [sb(f"wlo{i}", [128, KC, 512], F32R) for i in range(NSPL)]
        op0_at = top[0]
        OP0 = Operand(sb("op0h", [128, 16, 256], F32R), sb("op0l", [128, 16, 256], F32R))
        op1_at = top[0]
        OP1 = Operand(sb("op1h", [128, 16, 256], F32R), sb("op1l", [128, 16, 256], F32R))
        tmp = Pool([sb(f"tmp{i}", [128, 512]) for i in range(6)])
        ident = sb("ident", [128, 128])
        vat = sb("vat", [128, 112])
        vbt = sb("vbt", [128, 114])
        csil = sb("csil", [128, 32])
        abt = sb("abt", [128, 32, 2])
        acol = sb("acol", [128, 16, 2])
        a5 = sb("a5", [128, 512])
        ones = sb("ones", [128, 128])
        gqk = sb("gqk", [128, 2, 128])
        mhalf = sb("mhalf", [128, 4])
        stat = sb("stat", [128, 420])
        ss_all = sb("ss_all", [128, 3, 2, 4])
        big = top[0]
        assert big + 72 * 1024 <= nc.sbuf_usable_end, (big, nc.sbuf_usable_end)

        def bg(name, shape, kb, dt=F32):
            return at(name, shape, big + int(kb * 1024), dt)

        qb = bg("qb", [128, 8, 256], 0)
        kt1 = bg("kt1", [128, 2, 256], 8)
        kid = bg("kid", [128, 256], 10)
        v1 = bg("v1", [128, 2, 256], 11)
        wi = bg("wi", [128, 2, 16], 13)
        bt = bg("bt", [128, 8, 256], 14)
        pm = bg("pm", [128, 2, 4, 256], 14)
        sc = bg("sc", [128, 2, 256], 22)
        wk = bg("wk", [128, 2, 256], 24)
        mk = bg("mk", [128, 2, 256], 26)
        mx = bg("mx", [128, 16, 256], 28)
        pu = bg("pu", [128, 2, 512], 28)
        cu = bg("cu", [128, 4, 256], 32)
        pw = bg("pw", [128, 4, 2, 256], 36)
        junk0 = bg("junk0", [128, 2048], 36)
        cz = bg("cz", [128, 4, 258], 44)
        gt = [bg(f"gt{i}", [128, 4, 256], 44 + 4 * i) for i in range(2)]
        x0 = bg("x0", [128, 2, 2048], 52)
        YA = Operand(bg("yah", [128, 8, 256], 52, F32R), bg("yal", [128, 8, 256], 60, F32R))
        cm = bg("cm", [128, 2, 256], 68)
        oneh = bg("oneh", [128, 384], 70)
        flip = bg("flip", [128, 128], 70)
        vst = bg("vst", [128, 128], 71.5)
        vsu = bg("vsu", [128, 128], 44)
        erow = bg("erow", [128, 384], 22)
        ktc = bg("ktc", [128, 4, 256], 0)
        vc = bg("vc", [128, 2, 512], 4)
        X = bg("X", [128, 2, 2048], 8)
        macc = bg("macc", [128, 2, 2048], 24)
        HC = Operand(bg("hch", [128, 16, 256], 40, F32R), bg("hcl", [128, 16, 256], 56, F32R))
        g1b = bg("g1b", [128, 2048], 0)
        ctxs = at("ctxs", [128, 2, 2048], op0_at)
        ctxj = at("ctxj", [128, 2048], op0_at + 16384)
        zs = bg("zs", [128, 16, 256], 8)
        qt = bg("qt", [128, 12, 256], 24)
        ktx = bg("ktx", [128, 4, 256], 36)
        vx = bg("vx", [128, 2, 512], 40)
        rct = bg("rct", [128, 2, 512], 44)
        rst = bg("rst", [128, 2, 512], 48)
        ub = bg("ub", [128, 2, 512], 52)
        cst = bg("cst", [128, 2, 512], 56)
        cdt = bg("cdt", [128, 2, 128], 60)
        MG = Operand(bg("mgh", [128, 16, 256], 24, F32R), bg("mgl", [128, 16, 256], 40, F32R))
        ga = [bg(f"ga{i}", [128, 4, 256], 56 + 4 * i) for i in range(2)]
        gb = [bg(f"gb{i}", [128, 4, 256], 64 + 4 * i) for i in range(2)]
        gbc = bg("gbc", [128, 2048], 0)
        X2 = bg("X2", [128, 2, 2048], 8)
        fgb = at("fgb", [128, 2048], op1_at)
        junk2 = at("junk2", [128, 2048], op1_at + 8192)

        bank = [ctx.enter_context(nc.psum_tensor(f"ps{i}", [128, 512], F32)) for i in range(8)]
        main = Pool([(bank[0], bank[1]), (bank[2], bank[3])])
        rows = Pool([0])
        misc = Pool([bank[4], bank[5], bank[6], bank[7]])

        raw_sem = [p.new_sem(f"raw{i}") for i in range(NRAW)]
        R = {}
        tasks = []
        statn = [0]

        def load(name, dst, src, *tokens, eng=PO):
            R[name] = p.dma(eng, p.new_sem("d_" + name), dst, src, *tokens)
            return R[name]

        def col(n=2):
            i = statn[0]
            statn[0] += n
            assert statn[0] <= 420
            return stat[:, i:i + n]

        def step():
            for t in list(tasks):
                if t[1] > 0:
                    t[1] -= 1
                    continue
                try:
                    n = next(t[0])
                    t[1] = (n or 1) - 1
                except StopIteration:
                    tasks.remove(t)

        def until(cond, what=""):
            n = 0
            while not cond():
                step()
                n += 1
                assert n < 500, ("never ready", what)

        def start(gen):
            t = [gen, 0]
            try:
                n = next(gen)
                t[1] = (n or 1) - 1
                tasks.append(t)
            except StopIteration:
                pass

        def take(pool):
            while not pool.free:
                yield 1
            return pool.free.pop(0)

        def have(*names):
            while not all(n in R for n in names):
                yield 1

        def split(src, tok, hi, lo, *war, fast=False):
            if fast:
                t = p.op(DV, lambda e: e.tensor_copy(hi, src), tok, *war)
            else:
                t = p.op(AC, lambda e: e.activation(hi, src, ACT.Copy), tok, *war)
            return p.op(DV, lambda e: e.tensor_tensor(lo, src, hi.bitcast(F32), ALU.subtract), t, tok, *war)

        def rstd(dst, ss, tok, n=D):
            t = p.op(DV, lambda e: e.tensor_scalar(dst, ss, 1.0 / n, EPS, ALU.mult, ALU.add), tok)
            k = dst.shape[-1]
            return p.op(PO, lambda e: e.tensor_tensor(dst, dst, mhalf[:, 0:k], ALU.pow), t, R["mhalf"])

        def norm_rows(src, dst, junk, tok, *war):
            done = []
            sq = None
            for tt in range(2):
                s = col()
                t = sq = p.op(AC, lambda e, tt=tt, s=s: e.activation(dst[:, tt, :] if junk is None else junk, src[:, tt, :], ACT.Square, accum_out=s[:, 0:1]), tok[tt],
                              *war, sq)
                t = rstd(s[:, 1:2], s[:, 0:1], t)
                yield 1
                done.append(p.op(DV, lambda e, tt=tt, s=s: e.tensor_scalar(dst[:, tt, :], src[:, tt, :], s[:, 1:2], None, ALU.mult), t, *war))
            return done

        def to_operand(src, toks, a_of, b_of, op, *war, last=None):
            for kp in range(8):
                ps, fr = yield from take(misc)
                for i in range(4):
                    kt, tt = 2 * kp + i // 2, i % 2
                    f = lambda e, kt=kt, tt=tt, i=i, ps=ps: e.transpose(
                        ps[:, i * 128:(i + 1) * 128], src[:, tt, kt * 128:(kt + 1) * 128], ident[:, :])
                    if i < 3:
                        p.quiet(PE, f, fr, toks, R["ident"])
                    else:
                        t = p.op(PE, f, fr, toks, R["ident"])
                tm, ftm = yield from take(tmp)
                for j in range(2):
                    kt = 2 * kp + j
                    b = 0.0 if b_of is None else b_of(kt)
                    u = p.op(AC, lambda e, j=j, kt=kt, ps=ps, tm=tm, b=b: e.activation(
                        tm[:, j * 256:(j + 1) * 256], ps[:, j * 256:(j + 1) * 256], ACT.Identity,
                        bias=b, scale=a_of(kt)), t, ftm)
                misc.put(ps, u)
                src2 = tm[:, :].rearrange("p (k t) -> p k t", k=2)
                z = split(src2, u, op.hi[:, 2 * kp:2 * kp + 2, :], op.lo[:, 2 * kp:2 * kp + 2, :], op.read, *war, fast=True)
                tmp.put(tm, z)
                op.ready[2 * kp] = op.ready[2 * kp + 1] = z
                if kp % 2:
                    yield 1
            if last:
                R[last] = t

        R["mhalf"] = p.op(PO, lambda e: e.memset(mhalf[:, :], -0.5))
        load("x00", x0[:, 0, :], a["x"][0, 0:128, :], eng=SP)
        load("va1", vst[0:64, :], a["norm_gains"].rearrange("l g (r c) -> (l g r) c", c=128), eng=SP)
        load("va2", vst[64:112, :], a["b_gate"].rearrange("l g (r c) -> (l g r) c", c=128), eng=SP)
        load("ident", ident[:, :], a["k_ident"], eng=SP)
        load("x01", x0[:, 1, :], a["x"][0, 128:256, :], eng=SP)
        R["ones"] = p.op(PO, lambda e: e.memset(ones[:, :], 1.0))
        load("cm", cm[:, :, :], a["k_cm"].rearrange("p (t s) -> p t s", t=2))
        load("gq", gqk[:, 0, :], a["q_norm_g_2"].partition_broadcast(128).rearrange("p a n -> p (a n)"))
        load("gk", gqk[:, 1, :], a["k_norm_g_2"].partition_broadcast(128).rearrange("p a n -> p (a n)"))
        vec_rows = [("pool_scale", 8, "l (r c) -> (l r) c"), ("conv_w", 24, "l k (r c) -> (l k r) c"),
                    ("norm_g_2", 16, "l (r c) -> (l r) c"), ("q_norm_g_2", 1, None), ("k_norm_g_2", 1, None),
                    ("c_2", 16, "l (r c) -> (l r) c"), ("c_ctx_2", 16, "(r c) -> r c"), ("b_ada_2", 32, None)]
        PS0, CW0, NG0, CC0, BA0 = 0, 8, 32, 50, 82

        def setup():
            ps, fr = yield from take(misc)
            t = p.op(PE, lambda e: e.transpose(ps[:, 0:112], vst[0:112, :], ident[0:112, 0:112]), fr, R["va1"], R["va2"], R["ident"])
            R["vat"] = p.op(DV, lambda e: e.tensor_copy(vat[:, :], ps[:, 0:112]), t)
            misc.put(ps, R["vat"])
            yield 2
            r0 = 0
            for name, n, pat in vec_rows:
                src = a[name] if pat is None else a[name].rearrange(pat, c=128)
                if name == "b_ada_2":
                    src = src[:, 0:4096].rearrange("l (r c) -> (l r) c", c=128)
                load("vb_" + name, vsu[r0:r0 + n, :], src, eng=SP)
                r0 += n
            yield 3
            ps, fr = yield from take(misc)
            t = p.op(PE, lambda e: e.transpose(ps[:, 128:128 + 114], vsu[0:114, :], ident[0:114, 0:114]), fr, R["ident"], *[R["vb_" + v[0]] for v in vec_rows])
            R["vbt"] = p.op(DV, lambda e: e.tensor_copy(vbt[:, :], ps[:, 128:128 + 114]), t)
            misc.put(ps, R["vbt"])
            t = p.op(AC, lambda e: e.activation(csil[:, :], vbt[:, CC0:CC0 + 32], ACT.Sigmoid), R["vbt"])
            R["csil"] = p.op(DV, lambda e: e.tensor_tensor(csil[:, :], csil[:, :], vbt[:, CC0:CC0 + 32], ALU.mult), t)

        def setup_x():
            xn = yield from norm_rows(x0, x0, junk0[:, :], [R["x00"], R["x01"]])
            yield from have("vat")
            yield from to_operand(x0, xn, lambda kt: vat[:, kt:kt + 1], None, OP0, R["vat"], last="x0T")

        def done(job, *tokens):
            main.put(job.banks, *tokens)

        def ada(j):
            def run(job, t):
                if j >= 8:
                    yield from have("attn2")
                    _, fa = yield from take(rows)
                    tb = p.dma(PO, "d_a5", a5[0:1, :], a["b_ada_2"][0:1, 512 * j:512 * j + 512], fa)
                yield 1
                ps, fr = yield from take(misc)
                acc = job.acc
                if j < 8:
                    for m in range(4):
                        for f_ in range(2):
                            f = lambda e, m=m, f_=f_, ps=ps: e.matmul(ps[:, 2 * m + f_:2 * m + f_ + 1], acc[f_][:, 128 * m:128 * m + 128], ones[:, 0:1], start=True, stop=True)
                            t = p.op(PE, f, fr, job.acc_tok, R["ones"])
                    o = abt[:, 4 * j:4 * j + 4, :]
                    w = p.op(DV, lambda e: e.tensor_copy(o, ps[:, 0:8].rearrange("p (m f) -> p m f", m=4)), t)
                    for f_ in range(2):
                        v = p.op(DV, lambda e, f_=f_: e.tensor_tensor(abt[:, 4 * j:4 * j + 4, f_], abt[:, 4 * j:4 * j + 4, f_], vbt[:, BA0 + 4 * j:BA0 + 4 * j + 4], ALU.add), w, R["vbt"])
                else:
                    p.quiet(PE, lambda e: e.matmul(ps[:, :], ones[:, :], acc[0][:, :], start=True, stop=False), fr, job.acc_tok, R["ones"])
                    t = p.op(PE, lambda e: e.matmul(ps[:, :], ones[0:1, :], a5[0:1, :], start=False, stop=True), tb)
                    o = gbc[:, 512 * (j - 8):512 * (j - 7)]
                    v = p.op(DV, lambda e: e.tensor_copy(o, ps[:, :]), t, R["attn2"])
                    rows.put(0, t)
                R[f"ada{j}"] = v
                for x in acc:
                    tmp.put(x, t)
                misc.put(ps, v)
                if j == 7:
                    yield from have(*[f"ada{i}" for i in range(8)])
                    n = vbt[:, NG0:NG0 + 16]
                    for f in range(2):
                        v = p.op(DV, lambda e, f=f: e.scalar_tensor_tensor(acol[:, :, f], abt[:, 16:32, f], 1.0, n, ALU.add, ALU.mult), v, R["vbt"], *[R[f"ada{i}"] for i in range(8)])
                    R["acol"] = v
            return run

        def ev_copy(dst, name, *war):
            def run(job, t):
                nm = job.n // 128
                out_t = []
                for b in range((nm + 1) // 2):
                    k = min(2, nm - 2 * b)
                    o = dst[:, 2 * b:2 * b + k, :]
                    s = job.banks[b][:, 0:256 * k].rearrange("p (k t) -> p k t", k=k)
                    w = [R[x] for x in war]
                    if b % 2:
                        out_t.append(p.op(DV, lambda e, o=o, s=s: e.tensor_copy(o, s), t, w))
                    else:
                        out_t.append(p.op(AC, lambda e, o=o, s=s: e.activation(o, s, ACT.Copy), t, w))
                R[name] = out_t
                done(job, out_t)
                return
                yield
            return run

        def ep_kk(job, t):
            b0, b1 = job.banks
            u = p.op(AC, lambda e: e.activation(kt1[:, :, :], b0[:, :].rearrange("p (k t) -> p k t", k=2), ACT.Copy), t)
            v = p.op(AC, lambda e: e.activation(kid[:, :], b1[:, 0:256], ACT.Copy), t)
            R["k1"] = v
            done(job, v)
            return
            yield

        def ep_vw(job, t):
            o = []
            for tt in range(2):
                b = job.banks[tt]
                o.append(p.op(AC, lambda e, b=b, tt=tt: e.activation(v1[:, tt, :], b[:, 0:256], ACT.Copy), t))
                o.append(p.op(DV, lambda e, b=b, tt=tt: e.tensor_scalar(wi[:, tt, :], b[:, 256:272], 0.25, None, ALU.mult), o[-1]))
            R["v1"] = o
            done(job, o)
            start(indexer())
            return
            yield

        def indexer():
            yield from have("qi0", "qi1", "k1", "v1", "cm", "erow_w")
            first = [True, True]
            last = [None, None]
            units = [(1, par, i) for par in range(2) for i in range(4)] + [(0, par, i) for par in range(2) for i in range(2)]
            for tt, par, i in units:
                nh, nk = (2, 256) if tt else (4, 128)
                hs = [par + 2 * (nh * i + j) for j in range(nh)]
                ps, fr = yield from take(misc)
                for j, h in enumerate(hs):
                    lo = 64 * par
                    f = lambda e, j=j, h=h, ps=ps, lo=lo, tt=tt, nk=nk: e.matmul(
                        ps[:, j * nk:(j + 1) * nk], qb[lo:lo + 64, h // 2, tt * 128:tt * 128 + 128], kid[lo:lo + 64, 0:nk],
                        start=True, stop=True)
                    t = p.op(PE, f, fr, R["qi0"], R["qi1"], R["k1"])
                yield 1
                tm, ftm = yield from take(tmp)
                u = p.op(AC, lambda e, tm=tm, ps=ps: e.activation(tm[:, :], ps[:, :], ACT.Relu), t, ftm)
                misc.put(ps, u)
                for j, h in enumerate(hs):
                    s, r, w = sc[:, tt, 0:nk], tm[:, j * nk:(j + 1) * nk], wi[:, tt, h:h + 1]
                    if first[tt]:
                        first[tt] = False
                        v = p.op(DV, lambda e, s=s, r=r, w=w: e.tensor_scalar(s, r, w, None, ALU.mult), u, R["v1"], R["erow_w"])
                    else:
                        v = p.op(DV, lambda e, s=s, r=r, w=w: e.scalar_tensor_tensor(s, r, w, s, ALU.mult, ALU.add), u, last[tt])
                    last[tt] = v
                tmp.put(tm, v)
                R["qi_read"] = t
                yield 1
            R["qi_done"] = t
            for tt in range(2):
                nk = 128 * (tt + 1)
                s, w, m = sc[:, tt, 0:nk], wk[:, tt, 0:nk], mk[:, tt, 0:nk]
                c = cm[:, tt, 0:nk]
                v = p.op(DV, lambda e, s=s, c=c: e.tensor_tensor(s, s, c, ALU.add), last[tt])
                for r in range(8):
                    m8 = col(8)
                    i, o = (s, w) if r % 2 == 0 else (w, s)
                    v = p.op(DV, lambda e, m8=m8, i=i: e.max(m8, i), v)
                    v = p.op(DV, lambda e, m8=m8, i=i, o=o: e.match_replace(o, m8, i, -3e38), v)
                    if r % 2:
                        yield 1
                v = p.op(DV, lambda e, s=s, m=m: e.tensor_scalar(m, s, -2e38, BIG, ALU.is_le, ALU.mult), v)
                v = p.op(DV, lambda e, c=c, m=m: e.scalar_tensor_tensor(m, m, -BIG, c, ALU.add, ALU.add), v)
            R["mk"] = v

        def bias_table():
            load("oneh", oneh[0:32, :], a["k_onehot"])
            yield 12
            yield from take(rows)
            rb = load("relb", a5[0:32, 0:8], a["rel_bias"])
            ps, fr = yield from take(misc)
            t = p.op(PE, lambda e: e.matmul(ps[0:8, 0:384], a5[0:32, 0:8], oneh[0:32, :], start=True, stop=True), fr, rb, R["oneh"])
            rows.put(0, t)
            v = p.op(DV, lambda e: e.tensor_copy(erow[0:8, :], ps[0:8, 0:384]), t)
            misc.put(ps, v)
            w = load("erow", scratch_e, erow[0:8, :], v)
            R["erow_w"] = w
            R["erow_m"] = t

        def pool_ep(j):
            def run(job, t):
                o = []
                for tt in range(2):
                    b = job.banks[tt]
                    o.append(p.op(AC, lambda e, b=b, tt=tt: e.activation(pu[:, tt, :], b[:, :], ACT.Copy), t, R.get("pu_free"), R["x0T"]))
                done(job, o)
                yield 1
                for g in range(2):
                    gg = 2 * j + g
                    ps, fr = yield from take(misc)
                    for ct in range(2):
                        for st in range(2):
                            f = lambda e, ct=ct, st=st, g=g, gg=gg, ps=ps: e.matmul(
                                ps[:, ct * 256:ct * 256 + 256], pu[:, st, g * 256 + ct * 128:g * 256 + ct * 128 + 128],
                                pm[:, st, gg, :], start=(st == 0), stop=(st == 1))
                            u = p.op(PE, f, fr, o, R["pm"])
                    R["pu_free"] = u
                    yield 1
                    tm, ftm = yield from take(tmp)
                    v = p.op(AC, lambda e, tm=tm, ps=ps: e.activation(tm[:, :], ps[:, :], ACT.Copy), u, ftm)
                    misc.put(ps, v)
                    yield 1
                    ps, fr = yield from take(misc)
                    for dt in range(2):
                        for ct in range(2):
                            f = lambda e, ct=ct, dt=dt, gg=gg, ps=ps, tm=tm: e.matmul(
                                ps[:, dt * 256:dt * 256 + 256], pw[:, gg, ct, dt * 128:dt * 128 + 128],
                                tm[:, ct * 256:ct * 256 + 256], start=(ct == 0), stop=(ct == 1))
                            u = p.op(PE, f, fr, v, R["pw"])
                    yield 1
                    tn, ftn = yield from take(tmp)
                    for dt in range(2):
                        k = PS0 + 2 * gg + dt
                        w = p.op(AC, lambda e, dt=dt, k=k, ps=ps, tn=tn: e.activation(
                            tn[:, dt * 256:dt * 256 + 256], ps[:, dt * 256:dt * 256 + 256], ACT.Copy, scale=vbt[:, k:k + 1]), u, ftn, R["vbt"])
                    misc.put(ps, w)
                    tmp.put(tm, u)
                    z = split(tn[:, :].rearrange("p (k t) -> p k t", k=2), w, OP1.hi[:, 2 * gg:2 * gg + 2, :], OP1.lo[:, 2 * gg:2 * gg + 2, :])
                    tmp.put(tn, z)
                    OP1.ready[2 * gg] = OP1.ready[2 * gg + 1] = z
                    R[f"pool{gg}"] = u
                    yield 1
            return run

        def conv_u(job, t):
            o = []
            for b in range(2):
                s = job.banks[b][:, :].rearrange("p (k t) -> p k t", k=2)
                o.append(p.op(AC, lambda e, b=b, s=s: e.activation(cu[:, 2 * b:2 * b + 2, :], s, ACT.Copy), t, R.get("cu_free")))
            R["cu"] = o
            done(job, o)
            return
            yield

        def conv_c(blk):
            def run(job, t):
                if blk == 0:
                    R["cz0"] = p.op(DV, lambda e: e.memset(cz[:, :, 0:2], 0.0))
                o = []
                for b in range(2):
                    s = job.banks[b][:, :].rearrange("p (k t) -> p k t", k=2)
                    o.append(p.op(DV, lambda e, b=b, s=s: e.tensor_tensor(cz[:, 2 * b:2 * b + 2, 2:258], s, cu[:, 2 * b:2 * b + 2, :], ALU.mult), t, R["cu"], R.get("cz_free")))
                done(job, o)
                yield 1
                for c in range(4):
                    ct = 4 * blk + c
                    w = lambda k, ct=ct: vbt[:, CW0 + 8 * k + ct:CW0 + 8 * k + ct + 1]
                    v = p.op(DV, lambda e, c=c, w=w: e.tensor_scalar(cu[:, c, :], cz[:, c, 0:256], w(0), None, ALU.mult), o, R["cz0"], R["vbt"])
                    for k in (1, 2):
                        v = p.op(DV, lambda e, c=c, w=w, k=k: e.scalar_tensor_tensor(cu[:, c, :], cz[:, c, k:k + 256], w(k), cu[:, c, :], ALU.mult, ALU.add), v)
                    yield 1
                R[f"cy{blk}"] = v
                R["cz_free"] = v
            return run

        def conv_b(blk):
            def run(job, t):
                yield from have(f"cy{blk}")
                o = []
                for b in range(2):
                    tm, ftm = yield from take(tmp)
                    s = job.banks[b][:, :].rearrange("p (k t) -> p k t", k=2)
                    d = tm[:, :].rearrange("p (k t) -> p k t", k=2)
                    u = p.op(DV, lambda e, b=b, s=s, d=d: e.tensor_tensor(d, s, cu[:, 2 * b:2 * b + 2, :], ALU.mult), t, R[f"cy{blk}"], ftm)
                    o.append(u)
                    k = 8 + 4 * blk + 2 * b
                    z = split(d, u, OP1.hi[:, k:k + 2, :], OP1.lo[:, k:k + 2, :])
                    tmp.put(tm, z)
                    OP1.ready[k] = OP1.ready[k + 1] = z
                R["cu_free"] = u
                done(job, o)
            return run

        def attn1_table():
            yield from have("pool3", "erow_w")
            load("flip", flip[:, :], a["k_flip"], R["erow_m"])
            bts = []
            for i in range(4):
                tm, ftm = yield from take(tmp)
                load(f"bt{i}", tm[:, :].rearrange("p (h s) -> p h s", h=2), bass.AP(scratch_e.tensor, 768 * i, [[1, 128], [384, 2], [1, 256]]), R["erow_w"], ftm)
                ps, fr = yield from take(misc)
                t = p.op(PE, lambda e, ps=ps, tm=tm: e.matmul(ps[:, :], flip[:, :], tm[:, :], start=True, stop=True), fr, R["flip"], R[f"bt{i}"])
                tmp.put(tm, t)
                v = p.op(AC, lambda e, ps=ps, i=i: e.activation(bt[:, 2 * i:2 * i + 2, :], ps[:, :].rearrange("p (h s) -> p h s", h=2), ACT.Copy), t, R["pool3"])
                misc.put(ps, v)
                bts.append(v)
                yield 2
            R["bt"] = bts

        def attn1(hs):
            yield from have("mk", "q1", "q0", "x0T", "bt")
            for h in hs:
                ps, fr = yield from take(misc)
                g = h // 4
                for tt in range(2):
                    o = (0, 128, 384)
                    nk = 128 * (tt + 1)
                    f = lambda e, tt=tt, nk=nk, ps=ps, g=g, h=h, o=o: e.matmul(
                        ps[:, o[tt]:o[tt + 1]], qb[:, h, tt * 128:tt * 128 + 128], kt1[:, g, 0:nk], start=True, stop=True)
                    t = p.op(PE, f, fr, R["q0"], R["q1"], R["k1"])
                yield 1
                tm, ftm = yield from take(tmp)
                st = col(8)
                r0 = []
                for tt in range(2):
                    nk = 128 * (tt + 1)
                    L = tm[:, o[tt]:o[tt + 1]]
                    bb = bt[:, h, 128 * (1 - tt):256]
                    v = p.op(DV, lambda e, L=L, bb=bb, ps=ps, tt=tt, o=o: e.scalar_tensor_tensor(
                        L, ps[:, o[tt]:o[tt + 1]], ATT_SCALE, bb, ALU.mult, ALU.add), t, ftm, R["bt"])
                    r0.append(v)
                misc.put(ps, r0)
                for tt in range(2):
                    nk = 128 * (tt + 1)
                    L = tm[:, o[tt]:o[tt + 1]]
                    v = p.op(DV, lambda e, L=L, tt=tt, nk=nk, st=st: e.tensor_tensor_reduce(
                        L, L, mk[:, tt, 0:nk], 1.0, -3e38, ALU.add, ALU.max, st[:, tt:tt + 1]), r0, R["mk"])
                v = p.op(DV, lambda e, st=st: e.tensor_scalar(st[:, 2:4], st[:, 0:2], -1.0, None, ALU.mult), v)
                for tt in range(2):
                    L = tm[:, o[tt]:o[tt + 1]]
                    u = p.op(AC, lambda e, L=L, tt=tt, st=st: e.activation(
                        L, L, ACT.Exp, bias=st[:, 2 + tt:3 + tt], accum_out=st[:, 4 + tt:5 + tt]), v)
                v = p.op(DV, lambda e, st=st: e.reciprocal(st[:, 6:8], st[:, 4:6]), u)
                for tt in range(2):
                    L = tm[:, o[tt]:o[tt + 1]]
                    w = p.op(DV, lambda e, L=L, tt=tt, st=st: e.tensor_scalar(L, L, st[:, 6 + tt:7 + tt], None, ALU.mult), v, u)
                yield 2
                ps, fr = yield from take(misc)
                for i in range(3):
                    f = lambda e, i=i, ps=ps, tm=tm: e.transpose(ps[:, i * 128:i * 128 + 128], tm[:, (0, 128, 256)[i]:(0, 128, 256)[i] + 128], ident[:, :])
                    t = p.op(PE, f, fr, w)
                yield 1
                tn, ftn = yield from take(tmp)
                u = p.op(AC, lambda e, ps=ps, tn=tn: e.activation(tn[:, 0:384], ps[:, 0:384], ACT.Copy), t, ftn)
                misc.put(ps, u)
                tmp.put(tm, t)
                yield 2
                ps, fr = yield from take(misc)
                f = lambda e, ps=ps, tn=tn, g=g: e.matmul(ps[:, 0:256], v1[:, 0, g * 128:g * 128 + 128], tn[:, 0:256], start=True, stop=False)
                p.quiet(PE, f, fr, u, R["v1"])
                f = lambda e, ps=ps, tn=tn, g=g: e.matmul(ps[:, 128:256], v1[:, 1, g * 128:g * 128 + 128], tn[:, 256:384], start=False, stop=True)
                t = p.op(PE, f)
                tmp.put(tn, t)
                yield 1
                z = split(ps[:, 0:256], t, YA.hi[:, h, :], YA.lo[:, h, :], R["x0T"])
                misc.put(ps, z)
                YA.ready[h] = z
                yield 1
            R[f"attn1{hs[0]}"] = z
            if "attn10" in R and "attn11" in R:
                R["attn1"] = [R["attn10"], R["attn11"]]

        gate_tok = {}

        def gate_ep(n, c):
            def run(job, t):
                g = gt[(4 * n + c) % 2]
                fr = R.get(f"gtfree{(4 * n + c) % 2}")
                for m in range(4):
                    k = 64 + 16 * n + 4 * c + m
                    u = p.op(AC, lambda e, m=m, k=k: e.activation(
                        g[:, m, :], job.banks[m // 2][:, 256 * (m % 2):256 * (m % 2) + 256], ACT.Sigmoid, bias=vat[:, k:k + 1]),
                        t, R["vat"], fr, R["cy1"])
                gate_tok[n, c] = u
                if (n, c) == (2, 3):
                    R["gates_read"] = t
                done(job, u)
                return
                yield
            return run

        def branch_ep(n, c):
            def run(job, t):
                i = (4 * n + c) % 2
                g = gt[i]
                o = []
                for b in range(2):
                    s = job.banks[b][:, :].rearrange("p (k t) -> p k t", k=2)
                    m = mx[:, 4 * c + 2 * b:4 * c + 2 * b + 2, :]
                    gg = g[:, 2 * b:2 * b + 2, :]
                    if n == 0:
                        u = p.op(DV, lambda e, s=s, m=m, gg=gg: e.tensor_tensor(m, s, gg, ALU.mult), t, gate_tok[n, c], R["cu_free"], R["pool3"])
                        o.append(u)
                        continue
                    u = p.op(DV, lambda e, s=s, gg=gg: e.tensor_tensor(gg, s, gg, ALU.mult), t, gate_tok[n, c])
                    o.append(u)
                    v = p.op(DV, lambda e, m=m, gg=gg: e.tensor_tensor(m, m, gg, ALU.add), u, R[f"mx{c}"])
                    if n == 2:
                        k = 4 * c + 2 * b
                        z = split(m, v, OP1.hi[:, k:k + 2, :], OP1.lo[:, k:k + 2, :], OP1.read)
                        OP1.ready[k] = OP1.ready[k + 1] = z
                R[f"mx{c}"] = u if n == 0 else v
                R[f"gtfree{i}"] = R[f"mx{c}"]
                done(job, o)
                if (n, c) == (2, 3):
                    R["branches"] = [z]
                return
                yield
            return run

        def wout_ep(c):
            def run(job, t):
                if c == 0:
                    R["ssq"] = [None, None]
                ss = ss_t[0]
                o = []
                for tt in range(2):
                    tm, ftm = yield from take(tmp)
                    b = job.banks[tt]
                    u = p.op(AC, lambda e, b=b, tt=tt, tm=tm: e.activation(tm[:, :], b[:, :], ACT.Square, accum_out=ss[:, tt, c:c + 1]), t, ftm)
                    tmp.put(tm, u)
                    v = p.op(DV, lambda e, b=b, tt=tt: e.tensor_tensor(macc[:, tt, 512 * c:512 * c + 512], b[:, :], g1b[:, 512 * c:512 * c + 512], ALU.mult), u, R["g1b"])
                    o.append(v)
                done(job, o)
                if c == 3:
                    R["wout"] = v
                    start(after_mix())
            return run

        def after_mix():
            ss = ss_t[0]
            xs = []
            for tt in range(2):
                s = col()
                t = p.op(DV, lambda e, tt=tt, s=s: e.tensor_reduce(s[:, 0:1], ss[:, tt, 0:4], AX, ALU.add), R["wout"])
                t = rstd(s[:, 1:2], s[:, 0:1], t)
                yield 1
                xs.append(p.op(DV, lambda e, tt=tt, s=s: e.scalar_tensor_tensor(
                    X[:, tt, :], macc[:, tt, :], s[:, 1:2], X[:, tt, :], ALU.mult, ALU.add), t, R["xr"]))
            xn = yield from norm_rows(X, macc, None, xs)
            yield 3
            yield from to_operand(macc, xn, lambda kt: vat[:, 32 + kt:33 + kt], None, OP0, R["ctxT"], last="x1T")

        def context():
            yield from have("gates_read")
            ld = load("ctx", ctxs[:, :, :], a["ctx_2"].rearrange("b (t p) n -> p (b t) n", p=128), R["gates_read"])
            yield 4
            cn = yield from norm_rows(ctxs, ctxs, ctxj[:, :], [ld] * 2, R["gates_read"])
            yield 3
            yield from have("acol", "branches")
            w = [R["attn1"], R["branches"]]
            yield from to_operand(ctxs, cn, lambda kt: acol[:, kt, 1:2], lambda kt: abt[:, kt, 1:2], HC, R["acol"], *w, last="ctxT")

        def up_ep(blk, c):
            def run(job, t):
                for b in range(2):
                    tm, ftm = yield from take(tmp)
                    k = 4 * c + 2 * b
                    bk = job.banks[b]
                    u = p.op(AC, lambda e, bk=bk, tm=tm: e.activation(tm[:, :], bk[:, :], ACT.Relu), t, ftm)
                    if b == 0:
                        u0 = u
                    v = p.op(DV, lambda e, tm=tm: e.tensor_tensor(tm[:, :], tm[:, :], tm[:, :], ALU.mult), u)
                    z = split(tm[:, :].rearrange("p (k t) -> p k t", k=2), v, OP1.hi[:, k:k + 2, :], OP1.lo[:, k:k + 2, :], OP1.read)
                    tmp.put(tm, z)
                    OP1.ready[k] = OP1.ready[k + 1] = z
                done(job, u0, u)
            return run

        gains = {}

        def load_gain(c):
            tm, ftm = yield from take(tmp)
            src = a["norm_gains"][0, 3:4, 512 * c:512 * c + 512].partition_broadcast(128).rearrange("p a n -> p (a n)")
            gains[c] = (tm, load(f"g3{c}", tm[:, :], src, ftm))

        def down_ep(blk, c):
            def run(job, t):
                o = []
                if blk == 3 or (blk, c) == (2, 3):
                    n_ = c + 1 if blk == 3 else 0
                    if n_ < 4:
                        start(load_gain(n_))
                for tt in range(2):
                    b = job.banks[tt]
                    m = macc[:, tt, 512 * c:512 * c + 512]
                    if blk == 0:
                        yield from have("x1T")
                        u = p.op(AC, lambda e, b=b, m=m: e.activation(m, b[:, :], ACT.Copy), t, R["x1T"])
                    else:
                        u = p.op(DV, lambda e, b=b, m=m: e.tensor_tensor(m, b[:, :], m, ALU.add), t, R[f"mlp{c}"])
                    o.append(u)
                    if blk == 3:
                        tm, ftm = yield from take(tmp)
                        v = p.op(AC, lambda e, m=m, tt=tt, tm=tm: e.activation(tm[:, :], m, ACT.Square, accum_out=ss_t[1][:, tt, c:c + 1]), u, ftm)
                        tmp.put(tm, v)
                        R["ssq"] = v
                R[f"mlp{c}"] = o
                done(job, o)
                if blk == 3:
                    g, fg = gains.pop(c)
                    for tt in range(2):
                        m = macc[:, tt, 512 * c:512 * c + 512]
                        v = p.op(DV, lambda e, m=m, g=g: e.tensor_tensor(m, m, g[:, :], ALU.mult), R["ssq"], fg)
                    tmp.put(g, v)
                    R["g3m"] = v
                if (blk, c) == (3, 3):
                    start(after_mlp(o))
            return run

        def after_mlp(o):
            ss = ss_t[1]
            xs = []
            ts = []
            for tt in range(2):
                s = col()
                t = p.op(DV, lambda e, tt=tt, s=s: e.tensor_reduce(s[:, 0:1], ss[:, tt, 0:4], AX, ALU.add), R["ssq"], o)
                ts.append((s, rstd(s[:, 1:2], s[:, 0:1], t)))
            yield 1
            for tt in range(2):
                s, t = ts[tt]
                xs.append(p.op(DV, lambda e, tt=tt, s=s: e.scalar_tensor_tensor(
                    X[:, tt, :], macc[:, tt, :], s[:, 1:2], X[:, tt, :], ALU.mult, ALU.add), t, R["g3m"]))
                yield 1
            R["xw"] = p.dma(PO, p.new_sem("d_xw"), scratch_x.rearrange("(t p) n -> p t n", p=128), X[:, :, :], *xs)
            xn = yield from norm_rows(X, macc, None, xs)
            yield 3
            R["x2n"] = xn
            yield from to_operand(macc, xn, lambda kt: acol[:, kt, 0:1], lambda kt: abt[:, kt, 0:1], OP0, R["acol"], last="x2T")

        def qk_ep(kind, j):
            def run(job, t):
                g = gqk[:, 0 if kind == "q" else 1, :]
                rope = kind != "kc"
                dst = {"q": qt, "k": ktx, "kc": ktc}[kind]
                fin, outs = [], []
                for tt in range(2):
                    b = job.banks[tt]
                    t1, f1 = yield from take(tmp)
                    s = col(8)
                    for h in range(4):
                        sl = slice(128 * h, 128 * h + 128)
                        u = p.op(AC, lambda e, b=b, t1=t1, sl=sl, h=h, s=s: e.activation(t1[:, sl], b[:, sl], ACT.Square, accum_out=s[:, h:h + 1]), t, f1)
                    v = rstd(s[:, 4:8], s[:, 0:4], u, 128)
                    w = p.op(DV, lambda e, b=b, t1=t1: e.tensor_tensor(
                        t1[:, :].rearrange("p (h d) -> p h d", h=4), b[:, :].rearrange("p (h d) -> p h d", h=4),
                        g.unsqueeze(1).broadcast_to([128, 4, 128]), ALU.mult), u, R["gq"], R["gk"])
                    fin.append(w)
                    yield 1
                    for h in range(4):
                        sl = slice(128 * h, 128 * h + 128)
                        w = p.op(AC, lambda e, t1=t1, sl=sl, h=h, s=s: e.activation(t1[:, sl], t1[:, sl], ACT.Copy, scale=s[:, 4 + h:5 + h]), v, w)
                    if rope:
                        t2, f2 = yield from take(tmp)
                        sv = t1[:, :].rearrange("p (a h f) -> p a h f", h=2, f=32)
                        dv = t2[:, :].rearrange("p (a h f) -> p a h f", h=2, f=32)
                        rv = rst[:, tt, :].rearrange("p (a h f) -> p a h f", h=2, f=32)
                        y1 = p.op(DV, lambda e, sv=sv, dv=dv, rv=rv: e.tensor_tensor(dv[:, :, 0, :], sv[:, :, 1, :], rv[:, :, 0, :], ALU.mult), w, f2, R["rope"])
                        y2 = p.op(DV, lambda e, sv=sv, dv=dv, rv=rv: e.tensor_tensor(dv[:, :, 1, :], sv[:, :, 0, :], rv[:, :, 1, :], ALU.mult), w)
                        y3 = p.op(DV, lambda e, t1=t1, tt=tt: e.tensor_tensor(t1[:, :], t1[:, :], rct[:, tt, :], ALU.mult), y1, y2)
                        w = p.op(DV, lambda e, t1=t1, t2=t2: e.tensor_tensor(t1[:, :], t1[:, :], t2[:, :], ALU.add), y3)
                        tmp.put(t2, w)
                    outs.append((t1, w))
                done(job, fin)
                yield 3
                for tt in range(2):
                    t1, w = outs[tt]
                    ps, fr = yield from take(misc)
                    for h in range(4):
                        f = lambda e, h=h, ps=ps, t1=t1: e.transpose(ps[:, 128 * h:128 * h + 128], t1[:, 128 * h:128 * h + 128], ident[:, :])
                        u = p.op(PE, f, fr, w)
                    tmp.put(t1, u)
                    h0 = 4 * j
                    v = p.op(AC, lambda e, ps=ps, tt=tt, h0=h0: e.activation(
                        dst[:, h0:h0 + 4, 128 * tt:128 * tt + 128], ps[:, :].rearrange("p (h t) -> p h t", h=4), ACT.Copy), u, R.get("x2T"), R["branches"])
                    misc.put(ps, v)
                    if tt == 1:
                        R[f"{kind}t{j}"] = v
                    yield 1
            return run

        def v_ep(dst, name, *war):
            def run(job, t):
                o = []
                for tt in range(2):
                    b = job.banks[tt]
                    o.append(p.op(AC, lambda e, b=b, tt=tt: e.activation(dst[:, tt, :], b[:, :], ACT.Copy), t, [R[w] for w in war]))
                R[name] = o
                done(job, o)
                return
                yield
            return run

        def silu_ep(k0, name):
            def run(job, t):
                o = []
                for b in range(2):
                    s = job.banks[b][:, :].rearrange("p (k t) -> p k t", k=2)
                    d = zs[:, k0 + 2 * b:k0 + 2 * b + 2, :]
                    u = p.op(AC, lambda e, s=s, d=d: e.activation(d, s, ACT.Sigmoid), t, R["xw"], R["x2n"])
                    o.append(p.op(DV, lambda e, s=s, d=d: e.tensor_tensor(d, s, d, ALU.mult), u))
                R[name] = o
                done(job, o)
                return
                yield
            return run

        def fourier():
            yield from have("ub", "zb")
            for g in range(4):
                ps, fr = yield from take(misc)
                for tt in range(2):
                    f = lambda e, tt=tt, g=g, ps=ps: e.matmul(ps[:, :], ub[:, tt, 128 * g:128 * g + 128], cst[:, tt, :], start=(tt == 0), stop=(tt == 1))
                    t = p.op(PE, f, fr, R["ub"], R["fft"])
                yield 1
                tm, ftm = yield from take(tmp)
                u = p.op(AC, lambda e, ps=ps, tm=tm: e.activation(tm[:, :], ps[:, :], ACT.Copy), t, ftm)
                misc.put(ps, u)
                yield 1
                ps, fr = yield from take(misc)
                for i in range(2):
                    f = lambda e, i=i, ps=ps, tm=tm: e.matmul(ps[:, 0:256], cdt[:, i, :], tm[:, 256 * i:256 * i + 256], start=(i == 0), stop=(i == 1))
                    t = p.op(PE, f, fr, u)
                tmp.put(tm, t)
                yield 1
                tm, ftm = yield from take(tmp)
                v = p.op(DV, lambda e, ps=ps, tm=tm, g=g: e.tensor_tensor(tm[:, 0:256], ps[:, 0:256], zs[:, 12 + g, :], ALU.mult), t, ftm, R["zb"])
                misc.put(ps, v)
                z = split(tm[:, 0:256], v, OP1.hi[:, 12 + g, :], OP1.lo[:, 12 + g, :], OP1.read, R["x2n"])
                tmp.put(tm, z)
                OP1.ready[12 + g] = z
                yield 1
            R["fourier"] = [z, t]

        def attn2(hs):
            yield from have("kt0", "vx", "kct0", "vc")
            for h in hs:
                yield from have(f"qt{h // 4}")
                kv = h // 3
                sc2 = []
                for tt in range(2):
                    ps, fr = yield from take(misc)
                    for i, kk in enumerate((ktx, ktc)):
                        f = lambda e, i=i, kk=kk, ps=ps, tt=tt, h=h, kv=kv: e.matmul(
                            ps[:, 256 * i:256 * i + 256], qt[:, h, 128 * tt:128 * tt + 128], kk[:, kv, :], start=True, stop=True)
                        t = p.op(PE, f, fr, R[f"qt{h // 4}"], R["kt0"], R["kct0"])
                    sc2.append((ps, t))
                yield 1
                prob = []
                for ps, t in sc2:
                    st = col(4)
                    v = p.op(DV, lambda e, ps=ps, st=st: e.tensor_reduce(st[:, 0:1], ps[:, :], AX, ALU.max), t)
                    v = p.op(DV, lambda e, st=st: e.tensor_scalar(st[:, 1:2], st[:, 0:1], -ATT_SCALE, None, ALU.mult), v)
                    tm, ftm = yield from take(tmp)
                    u = p.op(AC, lambda e, ps=ps, st=st, tm=tm: e.activation(
                        tm[:, :], ps[:, :], ACT.Exp, bias=st[:, 1:2], scale=ATT_SCALE, accum_out=st[:, 2:3]), v, ftm)
                    misc.put(ps, u)
                    prob.append((tm, st, u))
                ws = []
                for tm, st, u in prob:
                    v = p.op(DV, lambda e, st=st: e.reciprocal(st[:, 3:4], st[:, 2:3]), u)
                    ws.append(p.op(DV, lambda e, st=st, tm=tm: e.tensor_scalar(tm[:, :], tm[:, :], st[:, 3:4], None, ALU.mult), v))
                yield 2
                tr = []
                for (tm, st, u), w in zip(prob, ws):
                    ps, fr = yield from take(misc)
                    for i in range(4):
                        f = lambda e, i=i, ps=ps, tm=tm: e.transpose(ps[:, 128 * i:128 * i + 128], tm[:, 128 * i:128 * i + 128], ident[:, :])
                        t = p.op(PE, f, fr, w)
                    tr.append((ps, tm, t))
                yield 1
                pts = []
                for ps, tm, t in tr:
                    u = p.op(AC, lambda e, ps=ps, tm=tm: e.activation(tm[:, :], ps[:, :], ACT.Copy), t)
                    misc.put(ps, u)
                    pts.append((tm, u))
                yield 2
                ps, fr = yield from take(misc)
                for tt in range(2):
                    tm, u = pts[tt]
                    for st_ in range(4):
                        vv = vx if st_ < 2 else vc
                        f = lambda e, st_=st_, tt=tt, tm=tm, vv=vv, ps=ps, kv=kv: e.matmul(
                            ps[:, 128 * tt:128 * tt + 128], vv[:, st_ % 2, 128 * kv:128 * kv + 128], tm[:, 128 * st_:128 * st_ + 128],
                            start=(st_ == 0), stop=(st_ == 3))
                        t = p.op(PE, f, fr, u, R["vx"], R["vc"])
                    tmp.put(tm, t)
                yield from have(f"za{h // 4}")
                yield 1
                tm, ftm = yield from take(tmp)
                v = p.op(DV, lambda e, ps=ps, tm=tm, h=h: e.tensor_tensor(tm[:, 0:256], ps[:, 0:256], zs[:, h, :], ALU.mult), t, ftm, R[f"za{h // 4}"])
                misc.put(ps, v)
                z = split(tm[:, 0:256], v, OP1.hi[:, h, :], OP1.lo[:, h, :], OP1.read, R["x2n"])
                tmp.put(tm, z)
                OP1.ready[h] = z
            R[f"attn2{hs[0] % 2}"] = [t, z]

        def after_attn2():
            yield from have("attn20", "attn21", "fourier")
            R["attn2"] = [R["attn20"], R["attn21"]]
            z = R["attn2"]
            load("xr2", X2[:, :, :], scratch_x.rearrange("(t p) n -> p t n", p=128), z, R["fourier"], R["xw"])

        def gate2_ep(buf, c, name):
            def run(job, t):
                yield from have("fourier")
                for m in range(4):
                    u = p.op(AC, lambda e, m=m: e.activation(
                        buf[c % 2][:, m, :], job.banks[m // 2][:, 256 * (m % 2):256 * (m % 2) + 256], ACT.Sigmoid),
                        t, R.get(f"{name}free{c % 2}"), R["fourier"], R["x2n"])
                R[f"{name}{c}"] = u
                done(job, u)
                return
                yield
            return run

        def pb_wait(c):
            def run(j, t):
                yield from have(f"gb{c}")
                o = []
                for b in range(2):
                    s = j.banks[b][:, :].rearrange("p (k t) -> p k t", k=2)
                    g = gb[c % 2][:, 2 * b:2 * b + 2, :]
                    o.append(p.op(DV, lambda e, s=s, g=g: e.tensor_tensor(g, s, g, ALU.mult), t, R[f"gb{c}"]))
                R[f"pb{c}"] = o
                done(j, o)
            return run

        def pa_wait(c):
            def run(j, t):
                yield from have(f"ga{c}", f"pb{c}", "attn2")
                o = []
                for b in range(2):
                    s = j.banks[b][:, :].rearrange("p (k t) -> p k t", k=2)
                    g = ga[c % 2][:, 2 * b:2 * b + 2, :]
                    m = gb[c % 2][:, 2 * b:2 * b + 2, :]
                    u = p.op(DV, lambda e, s=s, g=g: e.tensor_tensor(g, s, g, ALU.mult), t, R[f"ga{c}"])
                    o.append(u)
                    v = p.op(DV, lambda e, m=m, g=g: e.tensor_tensor(g, m, g, ALU.add), u, R[f"pb{c}"])
                    k = 4 * c + 2 * b
                    z = split(g, v, MG.hi[:, k:k + 2, :], MG.lo[:, k:k + 2, :], R["attn2"], R["fourier"])
                    MG.ready[k] = MG.ready[k + 1] = z
                R[f"gafree{c % 2}"] = R[f"gbfree{c % 2}"] = z
                done(j, o)
            return run

        def out2_ep(c):
            def run(job, t):
                o = []
                sums, fin = {}, {}
                if c == 0:
                    load("fgb", fgb[:, :], a["final_g_2"].partition_broadcast(128), OP1.read)
                for tt in range(2):
                    tm, ftm = yield from take(tmp)
                    b = job.banks[tt]
                    u = p.op(DV, lambda e, b=b, tm=tm: e.tensor_tensor(tm[:, :], b[:, :], gbc[:, 512 * c:512 * c + 512], ALU.mult), t, ftm, R[f"ada{8 + c}"])
                    o.append(u)
                    v = p.op(DV, lambda e, tm=tm, tt=tt: e.tensor_tensor(X2[:, tt, 512 * c:512 * c + 512], X2[:, tt, 512 * c:512 * c + 512], tm[:, :], ALU.add), u, R["xr2"])
                    w = p.op(AC, lambda e, tt=tt, tm=tm: e.activation(tm[:, :], X2[:, tt, 512 * c:512 * c + 512], ACT.Square, accum_out=ss_t[2][:, tt, c:c + 1]), v)
                    tmp.put(tm, w)
                    sums[tt] = w
                done(job, o)
                outs, rs = [], []
                for tt in range(2):
                    if c == 3:
                        s = col()
                        t = p.op(DV, lambda e, tt=tt, s=s: e.tensor_reduce(s[:, 0:1], ss_t[2][:, tt, 0:4], AX, ALU.add), sums[tt])
                        rs.append((s, rstd(s[:, 1:2], s[:, 0:1], t)))
                    fin[tt] = p.op(DV, lambda e, tt=tt: e.tensor_tensor(X2[:, tt, 512 * c:512 * c + 512], X2[:, tt, 512 * c:512 * c + 512], fgb[:, 512 * c:512 * c + 512], ALU.mult), sums[tt], R["fgb"])
                if c == 3:
                    for tt, hf in ((0, 0), (1, 0), (0, 1), (1, 1)):
                        s, t = rs[tt]
                        x = X2[:, tt, 1024 * hf:1024 * hf + 1024]
                        if tt == 0:
                            t2 = p.op(DV, lambda e, s=s, x=x: e.tensor_scalar(x, x, s[:, 1:2], None, ALU.mult), t, fin[tt])
                        else:
                            t2 = p.op(AC, lambda e, s=s, x=x: e.activation(x, x, ACT.Copy, scale=s[:, 1:2]), t, fin[tt])
                        outs.append(p.dma(SP, p.new_sem(f"d_out{tt}{hf}"), out[0].rearrange("(t p) n -> p t n", p=128)[:, tt, 1024 * hf:1024 * hf + 1024], x, t2))
                    p.wait(SP, *outs)
            return run

        ss_t = [ss_all[:, i, :, :] for i in range(3)]

        w_in, w_in2 = a["w_in"][0], a["w_in_2"][0]
        wbr, wg = a["w_branch"][0], a["w_gate"][0]
        p.new_sem("d_a5")
        jobs = []

        def J(mode, op, w, cols, ep, nkt=16, kt0=0, wk0=0, need=()):
            wv = w.rearrange("(k p) n -> p k n", p=128)[:, wk0:wk0 + nkt, :]
            return Job(mode, op, wv, kt0, nkt, cols, ep, need)

        def A(j):
            q = J("ada", Operand(None, None), a["w_ada_2"][0], [(512 * j, 512)], ada(j))
            q.nv = 2 if j < 8 else 1
            return q

        def W(op, w, c0, ep, **k):
            return J("W", op, w, [(c0, 512)], ep, **k)

        def T(op, w, c0, ep, n=512, **k):
            return J("T", op, w, [(c0, n)], ep, **k)

        def chunks(job):
            return [(job, k, min(KC, job.nkt - k)) for k in range(0, job.nkt, KC)]

        seq = []

        def add(*js):
            for j in js:
                seq.extend(chunks(j))

        def merge(main_jobs, side_jobs, every):
            m = [c for j in main_jobs for c in chunks(j)]
            s = list(side_jobs)
            for i, c in enumerate(m):
                seq.append(c)
                if i % every == every - 1 and s:
                    seq.append(s.pop(0))
            seq.extend(s)

        ph1 = [
            W(OP0, w_in, 5632, ev_copy(qb, "qi0", "x0T")),
            W(OP0, w_in, 6144, ev_copy(qb[:, 4:8, :], "qi1")),
            J("W", OP0, w_in, [(5120, 256), (6656, 64), (6656, 64)], ep_kk),
            J("T", OP0, w_in, [(5376, 256), (6720, 16)], ep_vw),
            T(OP0, w_in, 0, pool_ep(0)),
            T(OP0, w_in, 512, pool_ep(1)),
        ]
        for blk in range(2):
            ph1 += [W(OP0, w_in, 1024 + 512 * blk, conv_u), W(OP0, w_in, 2048 + 512 * blk, conv_c(blk)),
                    W(OP0, w_in, 3072 + 512 * blk, conv_b(blk))]
        ph1 += [W(OP0, w_in, 4096, ev_copy(qb, "q0", "qi_done")), W(OP0, w_in, 4608, ev_copy(qb[:, 4:8, :], "q1", "qi_done"))]
        for n, op, k0 in ((0, OP1, 0), (1, OP1, 8), (2, YA, 0)):
            for c in range(4):
                ph1 += [W(OP0, wg, 2048 * n + 512 * c, gate_ep(n, c)),
                        W(op, wbr[n], 512 * c, branch_ep(n, c), nkt=8, kt0=k0)]
        add(ph1[0])
        ADA = [c for j in range(8) for c in chunks(A(j))]
        n_ = 13
        merge(ph1[1:6], ADA[:n_], 3)
        add(*ph1[6:12])
        merge(ph1[12:], ADA[n_:], 3)
        add(*[T(OP1, a["w_out"][0], 512 * c, wout_ep(c)) for c in range(4)])
        add(T(HC, w_in2, 1536, qk_ep("kc", 0)))
        mid = []
        for blk in range(4):
            mid += [W(OP0, a["w_up"][0], 2048 * blk + 512 * c, up_ep(blk, c)) for c in range(4)]
            mid += [T(OP1, a["w_down"][0], 512 * c, down_ep(blk, c), wk0=16 * blk) for c in range(4)]
        add(*mid)
        add(T(HC, w_in2, 2048, v_ep(vc, "vc", "branches")))
        add(T(OP0, w_in2, 1536, qk_ep("k", 0)),
            T(OP0, w_in2, 2048, v_ep(vx, "vx", "x2T")),
            T(OP0, w_in2, 0, qk_ep("q", 0)),
            W(OP0, w_in2, 2560, silu_ep(0, "za0")),
            T(OP0, w_in2, 512, qk_ep("q", 1)),
            T(OP0, w_in2, 4096, v_ep(ub, "ub", "x2T")),
            W(OP0, w_in2, 4608, silu_ep(12, "zb")),
            T(OP0, w_in2, 1024, qk_ep("q", 2)),
            W(OP0, w_in2, 3072, silu_ep(4, "za1")),
            W(OP0, w_in2, 3584, silu_ep(8, "za2")))
        def g2(c):
            return [W(OP0, w_in2, 5120 + 512 * c, gate2_ep(ga, c, "ga")),
                    W(OP0, w_in2, 7168 + 512 * c, gate2_ep(gb, c, "gb")),
                    W(OP1, a["w_proj_b_2"][0], 512 * c, pb_wait(c), nkt=4, kt0=12)]

        def pa(c):
            return [W(OP1, a["w_proj_a_2"][0], 512 * c, pa_wait(c), nkt=12, kt0=0)]

        add(*g2(0))
        merge(g2(1) + pa(0) + pa(1) + g2(2) + pa(2) + g2(3) + pa(3), [c for j in range(8, 12) for c in chunks(A(j))], 2)
        add(*[T(MG, a["w_out_2"][0], 512 * c, out2_ep(c)) for c in range(4)])

        start(context())
        start(setup_x())
        start(setup())
        start(bias_table())
        load("pm", pm[:, :, :, :], a["k_pm"].rearrange("p (s g t) -> p s g t", s=2, g=4))

        def late_loads():
            yield from have("x0T")
            load("pw", pw[:, :, :, :], a["pool_w"].rearrange("l g (c p) d -> p (l g) c d", p=128), R["x0T"])
            yield from have("branches")
            w = [R["branches"], R["attn1"]]
            load("xr", X[:, :, :], a["x"].rearrange("b (t p) n -> p (b t) n", p=128), *w)
            load("g1b", g1b[:, :], a["norm_gains"][0, 1:2, :].partition_broadcast(128).rearrange("p a n -> p (a n)"), *w)
            yield from have("vc")
            while HCjobs_read() is None:
                yield 1
            w = [HC.read]
            R["rope1"] = load("rope_c", rct[:, :, :], a["k_rc"].rearrange("p (t n) -> p t n", t=2), *w)
            R["rope2"] = load("rope_s", rst[:, :, :], a["k_rs"].rearrange("p (t n) -> p t n", t=2), *w)
            R["rope"] = [R["rope1"], R["rope2"]]
            f1 = load("cs", cst[:, :, :], a["k_cs"].rearrange("p (t n) -> p t n", t=2), *w)
            f2 = load("cd", cdt[:, :, :], a["k_cd"].rearrange("p (t n) -> p t n", t=2), *w)
            R["fft"] = [f1, f2]
            start(attn2(range(0, 12, 2)))
            start(attn2(range(1, 12, 2)))
            start(after_attn2())
            start(fourier())

        def HCjobs_read():
            return HC.read if R.get("vc") else None

        start(late_loads())
        start(attn1_table())
        start(attn1(range(0, 8, 2)))
        start(attn1(range(1, 8, 2)))

        n = len(seq)
        lo_tok, pe_tok = {}, {}
        state = {"dma": 0, "split": 0, "pe": 0}
        order = [i for i, c in enumerate(seq) if c[0].mode != "ada"]
        place = {i: q for q, i in enumerate(order)}

        def emit_dma(i):
            job, k, nk = seq[i]
            w = [lo_tok[i - NRAW]] if i >= NRAW else []
            sl = i % NRAW
            o = 0
            for c0, cn in job.cols:
                t = p.dma(SP, raw_sem[sl], raw[sl][:, 0:nk, o:o + cn], job.w[:, k:k + nk, c0:c0 + cn], *w)
                o += cn
            return t

        dma_tok = {}

        def emit_split(i):
            job, k, nk = seq[i]
            if job.mode == "ada":
                if k == 0:
                    until(lambda: len(tmp.free) >= job.nv and "csil" in R, "acc")
                    got = [tmp.free.pop(0) for _ in range(job.nv)]
                    job.acc, job.acc_tok = [g[0] for g in got], [[g[1], R["csil"]] for g in got]
                for kk in range(nk):
                    for f_ in range(job.nv):
                        s_, c_, o_ = raw[i % NRAW][:, kk, :], csil[:, 16 * f_ + k + kk:16 * f_ + k + kk + 1], job.acc[f_]
                        if k + kk == 0:
                            f = lambda e, s_=s_, c_=c_, o_=o_: e.tensor_scalar(o_[:, :], s_, c_, None, ALU.mult)
                        else:
                            f = lambda e, s_=s_, c_=c_, o_=o_: e.scalar_tensor_tensor(o_[:, :], s_, c_, o_[:, :], ALU.mult, ALU.add)
                        lo_tok[i] = job.acc_tok[f_] = p.op(DV, f, job.acc_tok[f_], dma_tok[i])
                return
            q = place[i]
            w = [pe_tok[q - NSPL]] if q >= NSPL else []
            r, h, l = raw[i % NRAW], whi[q % NSPL], wlo[q % NSPL]
            r, h, l = (x[:, 0:nk, 0:job.n] for x in (r, h, l))
            t = p.op(AC, lambda e: e.activation(h, r, ACT.Copy), dma_tok[i], *w)
            lo_tok[i] = p.op(DV, lambda e: e.tensor_tensor(l, r, h.bitcast(F32), ALU.subtract), t, dma_tok[i], *w)

        def emit_pe(i):
            job, k, nk = seq[i]
            if job.mode == "ada":
                if k + nk == job.nkt:
                    start(job.epilogue(job, None))
                return
            if job.banks is None:
                pool = main
                until(lambda: pool.free, ("banks", i))
                job.banks, job.fr = pool.free.pop(0)
                for x in job.need:
                    until(lambda: x in R, x)
                job.wait0 = [job.fr] + [R[x] for x in job.need]
            op = job.op
            for kk in range(k, k + nk):
                until(lambda: job.kt0 + kk in op.ready, ("operand", i, kk))
            job.wait0 += [op.ready[job.kt0 + kk] for kk in range(k, k + nk)]
            w = job.wait0 + [lo_tok[i]]
            h, l = whi[place[i] % NSPL], wlo[place[i] % NSPL]
            last = None
            mms = []
            for kk in range(nk):
                kg = k + kk
                ka = job.kt0 + kg
                end = kg == job.nkt - 1
                if job.mode == "T":
                    for tt in range(2):
                        xh, xl = (x[:, ka, 128 * tt:128 * tt + 128] for x in (op.hi, op.lo))
                        o = job.banks[tt][:, 0:job.n]
                        mms.append((o, xh, h[:, kk, 0:job.n], kg == 0, False))
                        mms.append((o, xh, l[:, kk, 0:job.n], False, False))
                        mms.append((o, xl, h[:, kk, 0:job.n], False, end))
                else:
                    for m in range(job.n // 128):
                        o = job.banks[m // 2][:, 256 * (m % 2):256 * (m % 2) + 256]
                        wh, wl = (x[:, kk, 128 * m:128 * m + 128] for x in (h, l))
                        xh, xl = op.hi[:, ka, :], op.lo[:, ka, :]
                        mms.append((o, wh, xh, kg == 0 and m % 2 == 0, False))
                        mms.append((o, wh, xl, False, False))
                        mms.append((o, wl, xh, False, end))
            for q, (o, x, y, s, e_) in enumerate(mms):
                f = lambda e, o=o, x=x, y=y, s=s, e_=e_: e.matmul(o, x, y, start=s, stop=e_, skip_group_check=True)
                if q < len(mms) - 1:
                    p.quiet(PE, f, w)
                else:
                    last = p.op(PE, f, w)
            job.wait0 = []
            pe_tok[place[i]] = last
            if k + nk == job.nkt:
                job.op.read = last
                start(job.epilogue(job, last))

        step()
        step()
        for q in range(-AHEAD, len(order)):
            if q >= -2:
                step()
            while state["split"] < n and (q + AHEAD >= len(order) or state["split"] <= order[q + AHEAD]):
                j = state["split"]
                for d in range(state["dma"], min(n, j + NRAW)):
                    if d < NRAW or d - NRAW in lo_tok:
                        dma_tok[d] = emit_dma(d)
                        state["dma"] = d + 1
                emit_split(j)
                state["split"] = j + 1
            while q >= 0 and state["pe"] <= order[q]:
                emit_pe(state["pe"])
                state["pe"] += 1
        while state["pe"] < n:
            emit_pe(state["pe"])
            state["pe"] += 1
        k = 0
        while tasks:
            step()
            k += 1
            assert k < 1000
        for e in (PE, AC, DV):
            p.wait(SP, (e, p.count[e]))

        block = ctx.enter_context(nc.Block())

        def flush(eng, name):
            for f in p.q[name]:
                f(eng)

        @block.sync
        def _(eng):
            flush(eng, SP)

        @block.gpsimd
        def _(eng):
            flush(eng, PO)

        @block.scalar
        def _(eng):
            flush(eng, AC)

        @block.vector
        def _(eng):
            flush(eng, DV)

        @block.tensor
        def _(eng):
            flush(eng, PE)


_INS = ["x", "norm_gains", "w_in", "pool_w", "pool_scale", "conv_w", "rel_bias", "w_branch", "w_gate", "b_gate",
        "w_out", "w_up", "w_down", "c_2", "ctx_2", "c_ctx_2", "w_ada_2", "b_ada_2", "norm_g_2", "w_in_2",
        "q_norm_g_2", "k_norm_g_2", "w_proj_a_2", "w_proj_b_2", "w_out_2", "final_g_2"]


def kernel(**inputs):
    import concourse.bacc as _bacc
    from concourse.bass_utils import run_bass_kernel_spmd as _run

    nc = _bacc.Bacc("TRN2", target_bir_lowering=False, num_devices=1)
    arrays, aps = {}, {}
    given = {n: np.ascontiguousarray(inputs[n]) for n in _INS}
    given.update(constants())
    for name, v in given.items():
        arrays[f"in_{name}"] = v
        aps[name] = nc.dram_tensor(f"in_{name}", v.shape, mybir.dt.from_np(v.dtype), kind="ExternalInput").ap()
    out = nc.dram_tensor("out_dram", (1, 256, D), F32, kind="ExternalOutput").ap()
    se = nc.dram_tensor("scratch_e", (8, 384), F32).ap()
    sx = nc.dram_tensor("scratch_x", (256, D), F32).ap()
    program(nc, aps, out, se, sx)
    r = _run(nc, [arrays], core_ids=[0])
    return r.results[0]["out_dram"]
```
